# Optimizing a Trainium2 kernel written in Bass

```python
import math
import jax, jax.numpy as jnp
from jax import lax
import numpy as np

D_MODEL = 2048
BATCH = 1
SEQ = 256
DEPTH = 2

CHUNK = 64
N_MIXERS = 2
N_GDN_LAYERS = (DEPTH + 1) // 2
N_S5_LAYERS = DEPTH // 2
GDN_K_HEADS = 16
GDN_V_HEADS = 32
GDN_HEAD_K = 128
GDN_HEAD_V = 128
GDN_CONV = 4
GDN_KEY_DIM = GDN_K_HEADS * GDN_HEAD_K
GDN_VAL_DIM = GDN_V_HEADS * GDN_HEAD_V
GDN_CONV_DIM = 2 * GDN_KEY_DIM + GDN_VAL_DIM
GDN_PROJ_DIM = GDN_CONV_DIM + GDN_VAL_DIM + 2 * GDN_V_HEADS
S5_GROUP_CH = 16
S5_GROUPS = D_MODEL // S5_GROUP_CH
S5_STATE = 64
FF_DIM = 4 * D_MODEL
PLE_DIM = 256
NORM_EPS = 1e-6
L2_EPS = 1e-6

kernel_name = 'hybrid_gdn_s5_stream_encoder'

def rms_norm(x, g):
    xf = x.astype(jnp.float32)
    y = xf * lax.rsqrt(jnp.mean(xf * xf, axis=-1, keepdims=True) + NORM_EPS)
    return (y * g.astype(jnp.float32)).astype(x.dtype)

def l2_normalize(x):
    xf = x.astype(jnp.float32)
    return xf * lax.rsqrt(jnp.sum(xf * xf, axis=-1, keepdims=True) + L2_EPS)

def causal_depthwise_conv(x, w):
    k, c = w.shape
    return lax.conv_general_dilated(
        x, w[:, None, :].astype(x.dtype), window_strides=(1,), padding=[(k - 1, 0)],
        dimension_numbers=('NWC', 'WIO', 'NWC'), feature_group_count=c)

def gated_delta_rule_chunked(q, k, v, g, beta):
    bsz, seq, nh, dk = q.shape
    dv = v.shape[-1]
    nc = seq // CHUNK

    def to_chunks(t):
        return t.reshape(bsz, nc, CHUNK, nh, -1).transpose(0, 3, 1, 2, 4)

    q, k, v = to_chunks(q), to_chunks(k), to_chunks(v)
    g = to_chunks(g[..., None])[..., 0]
    beta = to_chunks(beta[..., None])[..., 0]
    gc = jnp.cumsum(g, axis=-1)
    idx = jnp.arange(CHUNK)
    causal = idx[:, None] >= idx[None, :]
    strict = idx[:, None] > idx[None, :]
    decay = jnp.where(causal, jnp.exp(jnp.minimum(gc[..., :, None] - gc[..., None, :], 0.0)), 0.0)
    kb = k * beta[..., None]
    m = jnp.where(strict, jnp.einsum('bhnid,bhnjd->bhnij', kb, k) * decay, 0.0)
    eye = jnp.eye(CHUNK, dtype=m.dtype)
    t_inv = lax.linalg.triangular_solve(eye + m, jnp.broadcast_to(eye, m.shape),
                                        left_side=True, lower=True, unit_diagonal=True)
    u = jnp.einsum('bhnij,bhnjd->bhnid', t_inv, v * beta[..., None])
    w = jnp.einsum('bhnij,bhnjd->bhnid', t_inv, kb * jnp.exp(gc)[..., None])
    qk = jnp.where(causal, jnp.einsum('bhnid,bhnjd->bhnij', q, k) * decay, 0.0)
    g_last = gc[..., -1]
    qg = q * jnp.exp(gc)[..., None]
    kd = k * jnp.exp(g_last[..., None] - gc)[..., None]

    def step(state, xs):
        qg_n, kd_n, w_n, u_n, qk_n, gl_n = xs
        v_new = u_n - jnp.einsum('bhck,bhkv->bhcv', w_n, state)
        o_n = (jnp.einsum('bhck,bhkv->bhcv', qg_n, state)
               + jnp.einsum('bhij,bhjv->bhiv', qk_n, v_new))
        state = state * jnp.exp(gl_n)[..., None, None] + jnp.einsum('bhck,bhcv->bhkv', kd_n, v_new)
        return state, o_n

    s0 = jnp.zeros((bsz, nh, dk, dv), jnp.float32)
    xs = tuple(jnp.moveaxis(t, 2, 0) for t in (qg, kd, w, u, qk, g_last))
    _, o = lax.scan(step, s0, xs)
    return o.transpose(1, 0, 3, 2, 4).reshape(bsz, seq, nh, dv)

def gdn_mixer(hn, w_in, conv_w, a_log, dt_bias, o_norm, w_out):
    bsz, seq, _ = hn.shape
    proj = hn @ w_in
    qkv = proj[..., :GDN_CONV_DIM]
    z = proj[..., GDN_CONV_DIM:GDN_CONV_DIM + GDN_VAL_DIM]
    b = proj[..., GDN_CONV_DIM + GDN_VAL_DIM:GDN_CONV_DIM + GDN_VAL_DIM + GDN_V_HEADS]
    a = proj[..., GDN_CONV_DIM + GDN_VAL_DIM + GDN_V_HEADS:]
    qkv = jax.nn.silu(causal_depthwise_conv(qkv, conv_w))
    q = qkv[..., :GDN_KEY_DIM].reshape(bsz, seq, GDN_K_HEADS, GDN_HEAD_K)
    k = qkv[..., GDN_KEY_DIM:2 * GDN_KEY_DIM].reshape(bsz, seq, GDN_K_HEADS, GDN_HEAD_K)
    v = qkv[..., 2 * GDN_KEY_DIM:].reshape(bsz, seq, GDN_V_HEADS, GDN_HEAD_V).astype(jnp.float32)
    rep = GDN_V_HEADS // GDN_K_HEADS
    q = jnp.repeat(l2_normalize(q), rep, axis=2) * (GDN_HEAD_K ** -0.5)
    k = jnp.repeat(l2_normalize(k), rep, axis=2)
    beta = jax.nn.sigmoid(b.astype(jnp.float32))
    g = -jnp.exp(a_log.astype(jnp.float32)) * jax.nn.softplus(a.astype(jnp.float32) + dt_bias.astype(jnp.float32))
    o = gated_delta_rule_chunked(q, k, v, g, beta)
    o = rms_norm(o, o_norm) * jax.nn.silu(z.reshape(bsz, seq, GDN_V_HEADS, GDN_HEAD_V).astype(jnp.float32))
    return o.reshape(bsz, seq, GDN_VAL_DIM).astype(hn.dtype) @ w_out

def s5_mixer(hn, w_in, lam_re, lam_im, log_step, b_re, b_im, c_re, c_im, d_skip, w_out):
    bsz, seq, _ = hn.shape
    u = (hn @ w_in).astype(jnp.float32)
    ug = u.reshape(bsz, seq, S5_GROUPS, S5_GROUP_CH).astype(jnp.complex64)
    lam = lax.complex(lam_re.astype(jnp.float32), lam_im.astype(jnp.float32))
    step = jnp.exp(log_step.astype(jnp.float32))[:, None]
    lam_bar = jnp.exp(lam * step)
    b_bar = lax.complex(b_re.astype(jnp.float32), b_im.astype(jnp.float32)) * ((lam_bar - 1.0) / lam)[..., None]
    bu = jnp.einsum('bsgc,gpc->bsgp', ug, b_bar)
    a = jnp.broadcast_to(lam_bar, bu.shape)

    def combine(left, right):
        a1, x1 = left
        a2, x2 = right
        return a1 * a2, a2 * x1 + x2

    _, states = lax.associative_scan(combine, (a, bu), axis=1)
    c = lax.complex(c_re.astype(jnp.float32), c_im.astype(jnp.float32))
    y = jnp.einsum('bsgp,gcp->bsgc', states, c).real.reshape(bsz, seq, D_MODEL)
    y = y + d_skip.astype(jnp.float32) * u
    h = jax.nn.gelu(y).astype(hn.dtype)
    vg = h @ w_out
    return vg[..., :D_MODEL] * jax.nn.sigmoid(vg[..., D_MODEL:])

def squared_relu_mlp(hn, w_up, w_down):
    return jnp.square(jax.nn.relu(hn @ w_up)) @ w_down

def setup_inputs(seed: int = 0) -> dict:
    key = jax.random.key(seed)
    ks = iter(jax.random.split(key, 40))

    def normal(shape, scale):
        return jax.random.normal(next(ks), shape, jnp.float32) * scale

    def gain(shape):
        return 1.0 + normal(shape, 0.02)

    x = normal((BATCH, SEQ, D_MODEL), 1.0)
    p = normal((DEPTH, BATCH, SEQ, PLE_DIM), 1.0)
    norm_mix = gain((DEPTH, D_MODEL))
    norm_mlp = gain((DEPTH, D_MODEL))
    norm_ple = gain((DEPTH, D_MODEL))
    norm_final = gain((D_MODEL,))
    gdn_w_in = normal((N_GDN_LAYERS, D_MODEL, GDN_PROJ_DIM), D_MODEL ** -0.5)
    gdn_conv_w = normal((N_GDN_LAYERS, GDN_CONV, GDN_CONV_DIM), GDN_CONV ** -0.5)
    gdn_a_log = jnp.log(jax.random.uniform(next(ks), (N_GDN_LAYERS, GDN_V_HEADS), jnp.float32, 1.0, 16.0))
    dt = jnp.exp(jax.random.uniform(next(ks), (N_GDN_LAYERS, GDN_V_HEADS), jnp.float32,
                                    math.log(1e-3), math.log(1e-1)))
    gdn_dt_bias = dt + jnp.log(-jnp.expm1(-dt))
    gdn_o_norm = gain((N_GDN_LAYERS, GDN_HEAD_V))
    gdn_w_out = normal((N_GDN_LAYERS, GDN_VAL_DIM, D_MODEL), GDN_VAL_DIM ** -0.5)
    s5_w_in = normal((N_S5_LAYERS, D_MODEL, D_MODEL), D_MODEL ** -0.5)
    n_idx = jnp.arange(S5_STATE, dtype=jnp.float32)
    s5_lam_re = -0.5 + normal((N_S5_LAYERS, S5_GROUPS, S5_STATE), 0.01)
    s5_lam_im = math.pi * n_idx + normal((N_S5_LAYERS, S5_GROUPS, S5_STATE), 0.01)
    s5_log_step = jax.random.uniform(next(ks), (N_S5_LAYERS, S5_GROUPS), jnp.float32,
                                     math.log(1e-3), math.log(1e-1))
    s5_b_re = normal((N_S5_LAYERS, S5_GROUPS, S5_STATE, S5_GROUP_CH), (2 * S5_GROUP_CH) ** -0.5)
    s5_b_im = normal((N_S5_LAYERS, S5_GROUPS, S5_STATE, S5_GROUP_CH), (2 * S5_GROUP_CH) ** -0.5)
    s5_c_re = normal((N_S5_LAYERS, S5_GROUPS, S5_GROUP_CH, S5_STATE), S5_STATE ** -0.5)
    s5_c_im = normal((N_S5_LAYERS, S5_GROUPS, S5_GROUP_CH, S5_STATE), S5_STATE ** -0.5)
    s5_d = normal((N_S5_LAYERS, D_MODEL), 1.0)
    s5_w_out = normal((N_S5_LAYERS, D_MODEL, 2 * D_MODEL), D_MODEL ** -0.5)
    mlp_w_up = normal((DEPTH, D_MODEL, FF_DIM), D_MODEL ** -0.5)
    mlp_w_down = normal((DEPTH, FF_DIM, D_MODEL), FF_DIM ** -0.5)
    ple_w_proj = normal((DEPTH, PLE_DIM, D_MODEL), PLE_DIM ** -0.5)
    ple_w_gate = normal((DEPTH, D_MODEL, D_MODEL), D_MODEL ** -0.5)
    return {'x': x, 'p': p, 'norm_mix': norm_mix, 'norm_mlp': norm_mlp, 'norm_ple': norm_ple,
            'norm_final': norm_final, 'gdn_w_in': gdn_w_in, 'gdn_conv_w': gdn_conv_w,
            'gdn_a_log': gdn_a_log, 'gdn_dt_bias': gdn_dt_bias, 'gdn_o_norm': gdn_o_norm,
            'gdn_w_out': gdn_w_out, 's5_w_in': s5_w_in, 's5_lam_re': s5_lam_re, 's5_lam_im': s5_lam_im,
            's5_log_step': s5_log_step, 's5_b_re': s5_b_re, 's5_b_im': s5_b_im, 's5_c_re': s5_c_re,
            's5_c_im': s5_c_im, 's5_d': s5_d, 's5_w_out': s5_w_out, 'mlp_w_up': mlp_w_up,
            'mlp_w_down': mlp_w_down, 'ple_w_proj': ple_w_proj, 'ple_w_gate': ple_w_gate}

def reference(x, p, norm_mix, norm_mlp, norm_ple, norm_final, gdn_w_in, gdn_conv_w, gdn_a_log,
              gdn_dt_bias, gdn_o_norm, gdn_w_out, s5_w_in, s5_lam_re, s5_lam_im, s5_log_step,
              s5_b_re, s5_b_im, s5_c_re, s5_c_im, s5_d, s5_w_out, mlp_w_up, mlp_w_down,
              ple_w_proj, ple_w_gate):
    h = x
    for i in range(DEPTH):
        j = i // N_MIXERS
        hn = rms_norm(h, norm_mix[i])
        if i % N_MIXERS == 0:
            mix = gdn_mixer(hn, gdn_w_in[j], gdn_conv_w[j], gdn_a_log[j], gdn_dt_bias[j],
                            gdn_o_norm[j], gdn_w_out[j])
        else:
            mix = s5_mixer(hn, s5_w_in[j], s5_lam_re[j], s5_lam_im[j], s5_log_step[j],
                           s5_b_re[j], s5_b_im[j], s5_c_re[j], s5_c_im[j], s5_d[j], s5_w_out[j])
        h = h + mix.astype(h.dtype)
        h = h + squared_relu_mlp(rms_norm(h, norm_mlp[i]), mlp_w_up[i], mlp_w_down[i]).astype(h.dtype)
        gate = jax.nn.sigmoid((rms_norm(h, norm_ple[i]) @ ple_w_gate[i]).astype(jnp.float32))
        h = h + (gate * (p[i] @ ple_w_proj[i]).astype(jnp.float32)).astype(h.dtype)
    return rms_norm(h, norm_final)


_drawn_inputs = setup_inputs


def setup_inputs(seed=0):
    import zlib

    import numpy as np

    out = dict(_drawn_inputs(seed))
    spreads = {}
    factors = {'norm_mix': 2.997,
     'norm_mlp': 2.721,
     'norm_ple': 64.0,
     'norm_final': 7.443,
     'gdn_o_norm': 4.522,
     's5_lam_re': 64.0,
     's5_lam_im': 25.416,
     's5_log_step': 29.608,
     's5_b_re': 35.664,
     's5_b_im': 35.736,
     's5_c_re': 35.952,
     's5_c_im': 34.84}
    for name, (base, spread) in spreads.items():
        noise = np.random.default_rng([zlib.crc32(name.encode()), seed]).standard_normal(out[name].shape)
        drawn = base * np.exp(spread * noise) if base else spread * noise
        out[name] = __import__('jax').numpy.asarray(drawn.astype(out[name].dtype))
    for name, factor in factors.items():
        out[name] = (out[name] * factor).astype(out[name].dtype)
    return out
```

```python
import math
from contextlib import ExitStack

import concourse.bass as bass
from concourse import mybir

ALU = mybir.AluOpType
ACT = mybir.ActivationFunctionType
F32 = mybir.dt.float32
F32R = mybir.dt.float32r
ds = bass.ds

P = 128
NT = 256
D = 2048
KT = D // P
FF = 4 * D
KH = 16
QUARTERS = 4
QK = KT // QUARTERS
EPS = 1e-6
MAGIC = 12582912.0

C_ID, C_ONE, C_U, C_SAME, C_M16, C_L1, C_L2, C_HALF, C_T, C_PAR = 0, 128, 256, 384, 512, 640, 768, 896, 1152, 1408
C_EPS = 1414

V_MIX, V_MLP, V_PLE, V_FIN, V_D = 0, 32, 64, 96, 112

H_BETA, H_GC, H_BEXP, H_KD, H_G, H_BHALF, H_GLAST, H_COLS = 0, 4, 8, 12, 16, 20, 24, 32

GDN_CHUNKS = 6 * KH
STAGES = 99
N_PARAMS = 20
TWO_PI_EXACT = 2 * math.pi
TWO_PI = 6.283185
PI_BELOW = 3.1415925
TP1, TP2 = 6.28125, 2029 / 2 ** 20
TP3 = 2 * math.pi - TP1 - TP2


class Sems:

    def __init__(self, nc, ctx):
        self._nc, self._ctx, self._made = nc, ctx, {}

    def __call__(self, name):
        if name not in self._made:
            self._made[name] = self._ctx.enter_context(self._nc.semaphore(name))
        return self._made[name]


def trunk(nc, t, out):
    with ExitStack() as ctx:
        S = Sems(nc, ctx)

        def sb(name, shape, dt=F32, scope=ctx):
            return scope.enter_context(nc.sbuf_tensor(name, shape, dt))

        bank = [ctx.enter_context(nc.psum_tensor(f"bank{i}", [P, 512], F32)) for i in range(8)]
        acc = bank[0:2]
        A, B, C, Dk, E, F = bank[2:8]

        act = sb("act", [P, KT, 2 * NT], F32R)
        g3 = ExitStack()
        sb("lower_half", [P, KT, 2 * NT], F32, g3)
        u = sb("u", [P, 2, NT], F32, g3)
        b_in = sb("b_in", [P, 2, 2, 4, 16], F32, g3)
        c_in = sb("c_in", [P, 2, 2, 64], F32, g3)
        b_t = sb("b_t", [P, 4, 64], F32, g3)
        b_blk = sb("b_blk", [P, 2, 4, 2, 16], F32, g3)
        c_blk = sb("c_blk", [P, 2, 2, 64], F32, g3)
        bcT = sb("bcT", [P, 4, P], F32, g3)
        tcol = sb("tcol", [P, NT + 6], F32, g3)
        turn = sb("turn", [P, 2, 2, NT], F32, g3)
        tq = sb("tq", [P, 2, 1], F32, g3)
        rot = sb("rot", [P, 2, 4, NT], F32, g3)
        st, rb, x1, x2 = (sb(n, [P, 2, NT], F32, g3) for n in ("st", "rb", "x1", "x2"))
        g3.close()
        mid = sb("mid", [P, 2 * KT, 2 * NT], F32R)
        raw = [sb(f"raw{i}", [P, KT * P]) for i in range(3)]
        w_hi = [sb(f"w_hi{i}", [P, KT * P], F32R) for i in range(2)]
        w_lo = [sb(f"w_lo{i}", [P, KT * P], F32R) for i in range(2)]
        eps = sb("eps", [P, 1])
        tiles_ = sb("tiles", [P, 6, NT])
        half = tiles_[:, 0:2, :]
        summed = tiles_[:, 2:4, :]
        tanh = tiles_[:, 4:6, :]
        cf = tiles_[:, 2:6, :].rearrange("p a n -> p (a n)").rearrange("p (c q) -> p c q", c=16)
        consts = sb("consts", [P, 256])
        ident, ones = consts[:, 0:128], consts[:, 128:256]
        vec = sb("vec", [P, 128])
        s5v = sb("s5v", [P, 5, 64])
        onorm = sb("onorm", [P, 1])

        g1 = ExitStack()

        def gs(name, shape, dt=F32):
            return sb(name, shape, dt, g1)

        masks = gs("masks", [P, 5, P])
        U, SAME, M16N, ML1, ML2 = (masks[:, i, :] for i in range(5))
        conv_w = gs("conv_w", [P, 4, 64])
        gt = gs("gt", [P, KH, H_COLS])
        g0 = ExitStack()
        xn = sb("xn", [P, 2, D], F32, g0)
        h0 = sb("h0", [P, KT, NT], F32, g0)
        rows = sb("rows", [P, 5, P], F32, g0)
        ba_w = raw[2][:, 0:KT * 64]
        ga = sb("ga", [P, 12, 64], F32, g0)
        stat = sb("stat", [P, 16], F32, g0)
        ls2 = sb("ls2", [P, 2], F32, g0)
        abias = sb("abias", [P, 3, 32], F32, g0)
        halfsel = sb("halfsel", [P, 2 * P], F32, g0)
        g0.close()
        pre = gs("pre", [P, 4, NT + 4])
        y = gs("y", [P, 4, NT])
        z = gs("z", [P, 2, NT])
        conv_f = gs("conv_f", [P, 4, 4])
        hs = gs("hs", [P, H_COLS])
        T = [gs(f"T{i}", [P, 4, P]) for i in range(6)]
        L1, L2, RT, Vb, Kbe, kd, qeT = (gs(n, [P, 4, P]) for n in ("L1", "L2", "RT", "Vb", "Kbe", "kd", "qeT"))
        state = gs("state", [P, 2, P])
        g1.close()
        sq, Mp, P2, P8, WT, osq = (T[0],) * 6
        rn, Pm, P4, Dm, orn = (T[1],) * 5
        D1, PT, P4T, nW, oy = (T[2],) * 5
        erow, P2T, VN = (T[3],) * 3
        qkn = T[4]
        qkT = T[5]

        g2 = ExitStack()

        def ls(name, shape, dt=F32):
            return sb(name, shape, dt, g2)

        raw.append(ls("raw3", [P, KT * P]))
        h = ls("h", [P, KT, NT])
        sqb = ls("sqb", [P, 2, NT])
        rms = ls("rms", [P, NT])
        normed = ls("normed", [P, 2, NT])
        tw, gl = sqb, normed
        pn = ls("pn", [P, 2, NT])
        pT = ls("pT", [P, 2, NT])
        wp = ls("wp", [P, 2, 2, P])
        row_out = ls("row_out", [P, 2, 512])
        g2.close()

        h_dram = nc.dram_tensor("h_scratch", (P, KT, NT), F32, kind="Internal").ap()
        w_in_d = t["gdn_w_in"][0].rearrange("(kt p) n -> p kt n", p=P)
        split4 = "(c kt p) n -> c p kt n"
        w_gout_d = t["gdn_w_out"][0].rearrange(split4, p=P, c=2)
        w_up_d = [t["mlp_w_up"][l].rearrange("(kt p) n -> p kt n", p=P) for l in range(2)]
        w_down_d = [t["mlp_w_down"][l].rearrange(split4, p=P, c=4) for l in range(2)]
        w_gate_d = [t["ple_w_gate"][l].rearrange("(kt p) n -> p kt n", p=P) for l in range(2)]
        w_pp_d = [t["ple_w_proj"][l].rearrange("(kt p) n -> p kt n", p=P) for l in range(2)]
        w_s5i_d = t["s5_w_in"][0].rearrange("(kt p) n -> p kt n", p=P)
        w_s5o_d = t["s5_w_out"][0].rearrange("(kt p) n -> p kt n", p=P)

        plan, n0, t0 = {}, GDN_CHUNKS, GDN_CHUNKS
        shapes = [("gout", 8, 4, 2)]
        for l in range(2):
            if l == 1:
                shapes += [("s5in", 4, 4, 4), ("s5out", 8, 4, 4)]
            for hf in range(2):
                shapes += [(f"up{l}{hf}", 8, 4, 4), (f"down{l}{hf}", 8, 4, 2)]
            shapes += [(f"ple{l}", 4, 4, 4)]
        if STAGES < 99:
            shapes = shapes[:STAGES]
        for name, rounds, chunks, tiles in shapes:
            plan[name] = (n0, t0, rounds, chunks, tiles)
            n0 += rounds * chunks
            t0 += rounds * tiles
        N_CHUNKS = n0

        def landed_before(n):
            if n < GDN_CHUNKS:
                return n // 3 + 1
            m = n - GDN_CHUNKS
            return m // 4 + 1 + (GDN_CHUNKS // 3 if m % 4 < 3 else 0)

        def raw_slot(n):
            return n % 3 if n < GDN_CHUNKS else (n - GDN_CHUNKS) % 4

        def load(sp, slot, src, split_done):
            if split_done is not None:
                sp.wait_ge(S("lo_ready"), split_done)
            sp.dma_start(raw[slot][:, :].rearrange("p (k n) -> p k n", k=KT), src).then_inc(S(f"raw_landed{slot}"), 16)

        def split_hi(eng, n, q, slot, landed, reused=True, par=None):
            if q == 0:
                eng.wait_ge(S(f"raw_landed{slot}"), 16 * landed)
            if reused:
                eng.wait_ge(S("weights_used"), 4 * n - 7 + q)
            c = slice(q * QK * P, (q + 1) * QK * P)
            eng.activation(w_hi[par][:, c], raw[slot][:, c], ACT.Copy).then_inc(S("hi_ready"), 1)

        def split_lo(eng, n, q, slot, par):
            eng.wait_ge(S("hi_ready"), 4 * n + q + 1)
            c = slice(q * QK * P, (q + 1) * QK * P)
            eng.tensor_tensor(w_lo[par][:, c], raw[slot][:, c], w_hi[par][:, c].bitcast(F32),
                              ALU.subtract).then_inc(S("lo_ready"), 1)

        def multiply(eng, n, q, par, tpar, rhs, k0=0, kend=KT, tile_free=None, last=False):
            if tile_free is not None:
                eng.wait_ge(S("acc_freed"), tile_free)
            eng.wait_ge(S("lo_ready"), 4 * n + q + 1)
            a = acc[tpar]
            for i in range(QK):
                kt = q * QK + i
                w = slice(kt * P, (kt + 1) * P)
                eng.matmul(a[:, :], w_hi[par][:, w], rhs[:, k0 + kt, :], start=(k0 + kt == 0), stop=False)
                mm = eng.matmul(a[:, 0:NT], w_lo[par][:, w], rhs[:, k0 + kt, 0:NT], start=False,
                                stop=(k0 + kt == kend - 1))
            mm.then_inc(S("weights_used"), 1)

        def half_copy(eng, n_end, tau, par, first=False):
            eng.wait_ge(S("weights_used"), 4 * n_end)
            if not first:
                eng.wait_ge(S("acc_freed"), tau - 1)
            eng.activation(half[:, par, :], acc[par][:, NT:2 * NT], ACT.Copy).then_inc(S("half_copied"), 1)

        def sum_halves(eng, tau, par, dst):
            eng.wait_ge(S("half_copied"), tau + 1)
            eng.tensor_tensor(dst, acc[par][:, 0:NT], half[:, par, :], ALU.add).then_inc(S("acc_freed"), 1)

        def norm_squares(eng, k, h_done):
            eng.wait_ge(S("h_updated"), 1 + h_done)
            with eng.Fori(0, KT // 2) as i:
                eng.wait_ge(S("sq_summed"), 1 + KT * k + 2 * i)
                for a in range(2):
                    eng.activation(sqb[:, a, :], h[:, ds(2 * i + a, 1), :], ACT.Square).then_inc(S("squared"), 1)
            eng.wait_ge(S("sq_summed"), 1 + KT * (k + 1))
            eng.activation(rms[:, :], F[:, 0:NT], ACT.Sqrt, scale=1.0 / D, bias=eps[:, 0:1]).then_inc(S("rms_root"), 1)

        def norm_sums(eng, k):
            for kt in range(KT):
                eng.wait_ge(S("squared"), KT * k + kt + 1)
                eng.matmul(F[:, 0:NT], ones, sqb[:, kt % 2, :], start=(kt == 0),
                           stop=(kt == KT - 1)).then_inc(S("sq_summed"), 1)

        def norm_scale(eng, k):
            eng.wait_ge(S("rms_root"), k + 1)
            eng.reciprocal(rms[:, :], rms[:, :]).then_inc(S("rms_ready"), 1)
            eng.wait_ge(S("rms_ready"), k + 1)

        def norm_apply_vector(eng, k, gain):
            norm_scale(eng, k)
            with eng.Fori(0, KT // 2) as i:
                if k:
                    eng.wait_ge(S("act_ready"), 1 + KT * k + 2 * i)
                else:
                    eng.wait_ge(S("act_ready"), 1 + 2 * i)
                for a in range(2):
                    eng.scalar_tensor_tensor(normed[:, a, :], h[:, ds(2 * i + a, 1), :], vec[:, ds(2 * i + (gain + a), 1)],
                                             rms[:, :], ALU.mult, ALU.mult).then_inc(S("normed"), 1)
                for a in range(2):
                    eng.wait_ge(S("norm_hi"), KT * k + 2 * i + a + 1)
                    eng.tensor_tensor(act[:, ds(2 * i + a, 1), NT:2 * NT], normed[:, a, :],
                                      act[:, ds(2 * i + a, 1), 0:NT].bitcast(F32), ALU.subtract).then_inc(S("act_ready"), 1)

        def norm_apply_scalar(eng, k):
            with eng.Fori(0, KT // 2) as i:
                for a in range(2):
                    eng.wait_ge(S("normed"), KT * k + 2 * i + a + 1)
                    eng.activation(act[:, ds(2 * i + a, 1), 0:NT], normed[:, a, :], ACT.Copy).then_inc(S("norm_hi"), 1)

        norm_of, h_done, upd = {}, {}, 0
        k = 0
        for name in plan:
            if name[:2] == "up" and name[3] == "0" or name[:3] == "ple" or name == "s5in":
                norm_of[name] = k
                k += 1
            h_done[name] = upd
            if name[:2] in ("go", "do", "pl") or name == "s5out":
                upd += 16
        K_FINAL, H_FINAL = k, upd
        gain_of = {"up00": V_MLP, "ple0": V_PLE, "s5in": V_MIX + 16, "up10": V_MLP + 16, "ple1": V_PLE + 16}

        block = ctx.enter_context(nc.Block())

        @block.sync
        def _(sp):
            sp.dma_start(xn[:, :, :], t["x"][0].rearrange("(b p) d -> p b d", p=P)).then_inc(S("x_in"), 16)
            par = [(consts[:, :], t["constants"][:, 0:256]),
                   (eps[:, :], t["constants"][:, C_EPS:C_EPS + 1]),
                   (masks[:, :, :], t["constants"][:, C_U:C_U + 640].rearrange("p (m q) -> p m q", m=5)),
                   (halfsel[:, :], t["constants"][:, C_HALF:C_HALF + 256]),
                   (rows[0:32, 0, :], t["norm_mix"].rearrange("l (k p) -> (l k) p", p=P)),
                   (rows[32:64, 0, :], t["norm_mlp"].rearrange("l (k p) -> (l k) p", p=P)),
                   (rows[64:96, 0, :], t["norm_ple"].rearrange("l (k p) -> (l k) p", p=P)),
                   (rows[96:112, 0, :], t["norm_final"].rearrange("(k p) -> k p", p=P)),
                   (rows[112:128, 0, :], t["s5_d"][0].rearrange("(k p) -> k p", p=P))]
            for tap in range(4):
                par.append((rows[64 * (tap % 2):64 * (tap % 2) + 64, 1 + tap // 2, :],
                            t["gdn_conv_w"][0][tap].rearrange("(k p) -> k p", p=P)))
            par += [(rows[0:64, 3, :], t["s5_lam_re"][0].rearrange("(q g) p -> q (g p)", g=2)),
                    (rows[64:128, 3, :], t["s5_lam_im"][0].rearrange("(q g) p -> q (g p)", g=2)),
                    (ls2[0:64, :], t["s5_log_step"][0].rearrange("(q g) -> q g", g=2)),
                    (abias[:, 0, :], t["gdn_a_log"].to_broadcast([P, 32])),
                    (abias[:, 1, :], t["gdn_dt_bias"].to_broadcast([P, 32])),
                    (onorm[:, :], t["gdn_o_norm"].rearrange("l (p o) -> (l p) o", o=1)),
                    (ba_w[:, :].rearrange("p (k n) -> p k n", k=KT), w_in_d[:, :, 12288:12352])]
            for dst, src in par:
                sp.dma_start(dst, src, allow_slow_non_contiguous=dst.shape[-1] == 1).then_inc(S("params_in"), 16)
            assert len(par) == N_PARAMS, len(par)
            for n, col in enumerate((0, 2048, 4096, 4096 + P)):
                if n == 2:
                    sp.wait_ge(S("ba_lo"), 1)
                load(sp, n % 3, w_in_d[:, :, col:col + P], 4 * (n - 2) if n >= 3 else None)
            sp.wait_ge(S("h0_ready"), 8)
            sp.dma_start(h_dram, h0[:, :, :]).then_inc(S("h_saved"), 16)
            with sp.Fori(0, KH - 1) as r:
                for c in range(6):
                    base = (8192, 8192 + P, P, 2048 + P, 4096 + 256, 4096 + 256 + P)[c]
                    step = 256 if c in (0, 1, 4, 5) else P
                    load(sp, (4 + c) % 3, w_in_d[:, :, ds(r * step + base, P)], 24 * r + 4 * (c + 2))
            for c in range(2):
                n = GDN_CHUNKS - 2 + c
                col = 8192 + 256 * (KH - 1) + P * c
                load(sp, n % 3, w_in_d[:, :, col:col + P], 4 * (n - 2))

            def gout_src(i, j):
                return w_gout_d[j % 2][:, :, ds(i * 256 + (j // 2) * P, P)] if not isinstance(i, int) else \
                    w_gout_d[j % 2][:, :, (2 * i + j // 2) * P:(2 * i + j // 2 + 1) * P]

            for j in range(4):
                n = GDN_CHUNKS + j
                if j == 3:
                    sp.wait_ge(S("mid_lo"), KH)
                    sp.wait_ge(S("h_saved"), 16)
                    sp.dma_start(h[:, :, :], h_dram).then_inc(S("h_loaded"), 16)
                    sp.dma_start(pn[:, :, :], t["p"][0][0].rearrange("(b p) e -> p b e", p=P)).then_inc(S("p_in"), 16)
                load(sp, j, gout_src(0, j), 4 * (n - 2))
            def b_and_c(ct, j, used):
                if used is not None:
                    sp.wait_ge(S("spread"), used)
                at = ds(ct, 1) if not isinstance(ct, int) else slice(ct, ct + 1)
                for ri, nm in enumerate(("re", "im")):
                    sp.dma_start(b_in[:, j % 2, ri, :, :], t[f"s5_b_{nm}"][0].rearrange(
                        "(c r g) p e -> c (g p) r e", g=2, r=4)[at][0]).then_inc(S(f"bc_in{j % 2}"), 16)
                    sp.dma_start(c_in[:, j % 2, ri, :], t[f"s5_c_{nm}"][0].rearrange(
                        "(c g) e p -> c (g e) p", g=8)[at][0]).then_inc(S(f"bc_in{j % 2}"), 16)

            def sub_loads(name, i, j):
                n0 = plan[name][0]
                col = lambda step, off: ds(i * step + off, P) if not isinstance(i, int) else slice(i * step + off, i * step + off + P)
                if name == "gout":
                    src = gout_src(i, j)
                elif name[:2] == "up":
                    src = w_up_d[int(name[2])][:, :, col(512, int(name[3]) * 4096 + j * P)]
                elif name[:4] == "down":
                    src = w_down_d[int(name[4])][2 * int(name[5]) + j % 2][:, :, col(256, (j // 2) * P)]
                elif name[:3] == "ple":
                    l = int(name[3])
                    src = w_gate_d[l][:, :, col(512, j * P)]
                    if l or not isinstance(i, int) or j >= 2:
                        sp.wait_ge(S("projected"), i * 4 + (16 * l + j - 1))
                    sp.dma_start(wp[:, j % 2, :, :], w_pp_d[l][:, :, col(512, j * P)]).then_inc(S(f"wp_in{j % 2}"), 16)
                elif name == "s5in":
                    src = w_s5i_d[:, :, col(512, j * P)]
                    if not isinstance(i, int):
                        b_and_c(i * 4 + j, j, i * 4 + j - 1)
                else:
                    src = w_s5o_d[:, :, col(256, (j % 2) * D + (j // 2) * P)]
                load(sp, j, src, i * 16 + (4 * (n0 + j) - (12 if name != "gout" else 8)))

            for name, (n0, t0, rounds, chunks, tiles) in plan.items():
                first = 0
                if name in ("ple0", "s5in"):
                    first = 1
                    for j in range(4):
                        sub_loads(name, 0, j)
                    if name == "s5in":
                        sp.wait_ge(S("h_updated"), 1 + h_done["s5in"])
                        sp.dma_start(tcol[:, :], t["constants"][:, C_T:C_T + 262]).then_inc(S("t_in"), 16)
                        for j in range(4):
                            b_and_c(j, j, j - 1 if j >= 2 else None)
                if name == "gout":
                    first = 1
                with sp.Fori(first, rounds) as i:
                    for j in range(4):
                        sub_loads(name, i, j)
                if name == "ple0" and "ple1" in plan:
                    sp.wait_ge(S("p_turned"), 1)
                    sp.dma_start(pn[:, :, :], t["p"][1][0].rearrange("(b p) e -> p b e", p=P)).then_inc(S("p_in"), 16)
            for i in range(8):
                sp.wait_ge(S("row_ready"), i + 1)
                sp.dma_start(out[0].rearrange("(b p) d -> b p d", p=P)[i // 4][:, (i % 4) * 512:(i % 4 + 1) * 512],
                             row_out[:, i % 2, :]).then_inc(S(f"stored{i % 2}"), 16)
            for a in range(2):
                sp.wait_ge(S(f"stored{a}"), 64)

        @block.tensor
        def _(pe):
            for name in ("sq_summed", "bc_turned", "y_done", "x1_used"):
                pe.sem_inc(S(name), 1)
            pe.wait_ge(S("params_in"), 16 * N_PARAMS)
            for i in range(4):
                mm = pe.transpose(A[:, i * P:(i + 1) * P], rows[:, i, :], ident)
            mm.then_inc(S("vectors_turned"), 1)
            pe.wait_ge(S("steps_ready"), 1)
            pe.transpose(B[:, 0:64], rows[0:64, 4, :], ident[0:64, 0:64]).then_inc(S("vectors_turned"), 1)
            for again in range(2):
                if again:
                    pe.wait_ge(S("x_scaled"), 2)
                else:
                    pe.wait_ge(S("x_in"), 16)
                for g in range(8):
                    bk = (C, Dk, E, F)[g % 4]
                    if again:
                        pe.wait_ge(S("act_ready0"), 2 * (g - 4) + 2 if g >= 4 else 0)
                        pe.wait_ge(S("h0_ready"), 8)
                    elif g >= 4:
                        pe.wait_ge(S("h0_ready"), g - 3)
                    for a in range(2):
                        for b in range(2):
                            mm = pe.transpose(bk[:, a * NT + b * P:a * NT + (b + 1) * P],
                                              xn[:, b, (2 * g + a) * P:(2 * g + a + 1) * P], ident)
                    mm.then_inc(S("x_turned"), 1)
            pe.wait_ge(S("act_ready0"), KT)
            pe.wait_ge(S("ba_lo"), 1)
            pe.wait_ge(S("vectors_ready"), 2)
            bh = mid[:, 0:2, :].rearrange("p a n -> p (a n)").rearrange("p (k n) -> p k n", k=KT)
            bl = mid[:, 2:4, :].rearrange("p a n -> p (a n)").rearrange("p (k n) -> p k n", k=KT)
            for b in range(2):
                for kt in range(KT):
                    x_hi, x_lo = act[:, kt, b * P:(b + 1) * P], act[:, kt, NT + b * P:NT + (b + 1) * P]
                    pe.matmul(A[:, b * 64:(b + 1) * 64], x_hi, bh[:, kt, :], start=(kt == 0), stop=False)
                    pe.matmul(A[:, b * 64:(b + 1) * 64], x_lo, bh[:, kt, :], start=False, stop=False)
                    mm = pe.matmul(A[:, b * 64:(b + 1) * 64], x_hi, bl[:, kt, :], start=False, stop=(kt == KT - 1))
            mm.then_inc(S("ba_done"), 1)
            for n in range(4):
                for q in range(QUARTERS):
                    multiply(pe, n, q, n % 2, n % 2, act, tile_free=(n - 1) if (n >= 2 and q == 0) else None)
                if n == 0:
                    pe.wait_ge(S("setup_vectors"), 7)
                    g_all = ga[:, 8, :]
                    pe.matmul(B[:, 0:64], U, g_all, start=True, stop=True)
                    pe.matmul(B[:, 64:128], SAME, g_all, start=True, stop=True)
                    for hc in range(2):
                        mm = pe.matmul(B[:, 128 + 64 * hc:192 + 64 * hc], halfsel[:, hc * P:(hc + 1) * P], g_all,
                                       start=True, stop=True)
                    mm.then_inc(S("gc_done"), 1)

            def four(bk, lhs, rhs, name, turn_=False):
                for m in range(4):
                    if turn_:
                        mm = pe.transpose(bk[:, m * P:(m + 1) * P], lhs[:, m, :], ident)
                    else:
                        mm = pe.matmul(bk[:, m * P:(m + 1) * P], lhs[:, m, :], rhs[:, m, :], start=True, stop=True)
                mm.then_inc(S(name), 1)

            def out_chunk(r, c):
                b, lo = c // 2, 64 * (c % 2)
                for hd in range(2):
                    dst = B[:, hd * NT + 64 * c:hd * NT + 64 * (c + 1)]
                    if c:
                        pe.matmul(dst, state[:, hd, :], qeT[:, 2 * b + hd, lo:lo + 64], start=True, stop=False)
                    mm = pe.matmul(dst, VN[lo:lo + 64, 2 * b + hd, :], qkT[lo:lo + 64, 2 * b + hd, lo:lo + 64],
                                   start=(c == 0), stop=True)
                return mm

            def state_add(c):
                b, lo = c // 2, 64 * (c % 2)
                for hd in range(2):
                    mm = pe.matmul(C[:, hd * P:(hd + 1) * P], kd[lo:lo + 64, 2 * b + hd, :],
                                   VN[lo:lo + 64, 2 * b + hd, :], start=True, stop=True)
                mm.then_inc(S("kv_done"), 1)

            def state_read(r, c):
                b, lo = c // 2, 64 * (c % 2)
                pe.wait_ge(S("state_ready"), 3 * r + c)
                for hd in range(2):
                    mm = pe.matmul(A[lo:lo + 64, hd * P:(hd + 1) * P], nW[:, 2 * b + hd, lo:lo + 64],
                                   state[:, hd, :], start=True, stop=True)
                mm.then_inc(S("ws_done"), 1)

            def core(r, s):
                w = lambda name, k=1, o=1: pe.wait_ge(S(name), k * r + o)
                if s == 0:
                    w("hs_ready")
                    for m in range(4):
                        mm = pe.matmul(C[:, m * P:(m + 1) * P], hs[:, H_G + m:H_G + m + 1].to_broadcast([P, P]), U,
                                       start=True, stop=True)
                    mm.then_inc(S("gcrow"), 1)
                elif s == 1:
                    w("sq_ready")
                    pe.matmul(A[:, :], ones, sq[:, :, :].rearrange("p m q -> p (m q)"), start=True, stop=True).then_inc(S("ssum"), 1)
                elif s == 2:
                    w("qkn_ready")
                    kq = qkn[:, :, :].rearrange("p (a b) q -> p a b q", a=2)
                    for b in range(2):
                        mm = pe.matmul(B[:, b * NT:(b + 1) * NT], kq[:, 1, b, :], kq[:, :, b, :], start=True, stop=True)
                    mm.then_inc(S("attn_done"), 1)
                    pe.wait_ge(S("gated"), 6 * r + 4)
                    for b in range(2):
                        for hd in range(2):
                            pe.transpose(Dk[:, (2 * b + hd) * P:(2 * b + hd + 1) * P], y[:, 2 + hd, b * P:(b + 1) * P], ident)
                        mm = pe.transpose(E[:, b * P:(b + 1) * P], kq[:, 1, b, :], ident)
                    mm.then_inc(S("vk_turned"), 1)
                elif s == 3:
                    w("P_ready")
                    four(A, Pm, None, "PT_turned", True)
                elif s == 4:
                    w("PT_ready")
                    four(C, PT, Pm, "P2_done")
                    four(F, Pm, PT, "P2T_done")
                elif s == 5:
                    w("P2_ready")
                    w("RT_ready", 6, 1)
                    four(A, P2, RT, "R_done")
                    w("P2T_ready")
                    four(C, P2T, P2, "P4_done")
                    four(F, P2, P2T, "P4T_done")
                elif s == 6:
                    w("P4_ready")
                    w("RT_ready", 6, 2)
                    four(A, P4, RT, "R_done")
                    w("P4T_ready")
                    four(C, P4T, P4, "P8_done")
                elif s == 7:
                    w("P8_ready")
                    w("RT_ready", 6, 3)
                    four(A, P8, RT, "R_done")
                elif s == 8:
                    w("RT_ready", 6, 4)
                    four(C, RT, None, "D1_turned", True)
                elif s == 9:
                    w("L_ready")
                    four(A, L1, RT, "W1_done")
                elif s == 10:
                    w("Dm_ready", 2)
                    w("WT_ready", 2)
                    four(C, Dm, WT, "R_done")
                elif s == 11:
                    w("RT_ready", 6, 5)
                    four(A, RT, None, "D2_turned", True)
                    four(F, L2, RT, "W2_done")
                elif s == 12:
                    w("Dm_ready", 2, 2)
                    w("WT_ready", 2, 2)
                    four(C, Dm, WT, "R_done")
                elif s == 13:
                    w("RT_ready", 6, 6)
                    w("Vb_ready")
                    four(A, RT, Vb, "U_done")
                    w("Kbe_ready")
                    four(F, Kbe, RT, "W_done")
                elif s == 14:
                    w("VN_ready")
                    w("qkT_ready")
                    out_chunk(r, 0)
                    w("kd_ready")
                    state_add(0)
                elif s in (15, 17, 19):
                    if s == 15:
                        w("nW_ready")
                    state_read(r, (s - 13) // 2)
                elif s in (16, 18, 20):
                    c = (s - 14) // 2
                    if c == 1:
                        w("qeT_ready")
                    pe.wait_ge(S("vn_ready"), 3 * r + c)
                    mm = out_chunk(r, c)
                    if c < 3:
                        state_add(c)
                    else:
                        mm.then_inc(S("ot_done"), 1)
                elif s == 21:
                    w("osq_ready")
                    pe.matmul(E[:, :], ones, osq[:, :, :].rearrange("p m q -> p (m q)"), start=True, stop=True).then_inc(S("osum_done"), 1)

            def head(r, last):
                for s in range(24):
                    if s < 8 or not last:
                        c, q = s // 4, s % 4
                        n = 6 * r + 4 + c
                        multiply(pe, n, q, c % 2, c % 2, act, tile_free=n - 1 if q == 0 else None)
                    core(r, s)

            with pe.Fori(0, KH - 1) as r:
                head(r, False)
            head(KH - 1, True)

            def turn_p(l):
                pe.wait_ge(S("p_in"), 16 * (l + 1))
                for e in range(2):
                    for b in range(2):
                        mm = pe.transpose(E[:, e * NT + b * P:e * NT + (b + 1) * P], pn[:, b, e * P:(e + 1) * P], ident)
                mm.then_inc(S("p_turned"), 1)

            def s5_in_tile(i, j, more, n0, t0):
                ct = 4 * i + j
                pe.wait_ge(S("spread"), ct + 1)
                for a in range(2):
                    pe.transpose(B[:, a * P:(a + 1) * P], b_blk[:, a, :, :, :].rearrange("p r g e -> p (r g e)"), ident)
                for a in range(2):
                    mm = pe.transpose(B[:, (2 + a) * P:(3 + a) * P], c_blk[:, a, :, :].rearrange("p g e -> p (g e)"), ident)
                mm.then_inc(S("bc_turned"), 1)
                pe.wait_ge(S("bcT_ready"), ct + 1)
                pe.wait_ge(S("acc_freed"), t0 + ct + 1)
                for r4 in range(4):
                    bk = (C, Dk, E, F)[r4]
                    for a in range(2):
                        mm = pe.matmul(bk[:, a * NT:(a + 1) * NT], bcT[32 * r4:32 * r4 + 32, a, :],
                                       u[32 * r4:32 * r4 + 32, j % 2, :], start=True, stop=True)
                    mm.then_inc(S("bu_done"), 1)
                for r4 in range(4):
                    if more:
                        n = n0 + ct + 1
                        multiply(pe, n, r4, (j + 1) % 2, (j + 1) % 2, act,
                                 tile_free=t0 + ct if r4 == 0 else None)
                    pe.wait_ge(S("x1_ready"), 4 * ct + r4 + 1)
                    if r4 == 0:
                        pe.wait_ge(S("gelu_in"), 1 + ct)
                    dst = A[32 * r4:32 * r4 + 32, 0:NT]
                    cre, cim = bcT[:, 2, 32 * r4:32 * r4 + 32], bcT[:, 3, 32 * r4:32 * r4 + 32]
                    pe.matmul(dst, cre, x1[:, 0, :], start=True, stop=False)
                    pe.matmul(dst, cim, x1[:, 1, :], start=False, stop=False).then_inc(S("x1_used"), 1)
                    pe.wait_ge(S("x2_ready"), 1 + 4 * ct + r4 + 1)
                    pe.matmul(dst, cre, x2[:, 1, :], start=False, stop=False)
                    pe.matmul(dst, cim, x2[:, 0, :], start=False, stop=True).then_inc(S("y_done"), 1)

            for name, (n0, t0, rounds, chunks, tiles) in plan.items():
                if name in norm_of:
                    k = norm_of[name]
                    norm_sums(pe, k)
                if name[:3] == "ple":
                    turn_p(int(name[3]))
                    pe.wait_ge(S("pT_ready"), int(name[3]) + 1)
                if name == "s5in":
                    for q in range(QUARTERS):
                        pe.wait_ge(S("act_ready"), 1 + KT * norm_of[name] + QK * (q + 1))
                        multiply(pe, n0, q, 0, 0, act, tile_free=t0 - 1 if q == 0 else None)
                    with pe.Fori(0, 3) as i:
                        for j in range(4):
                            s5_in_tile(i, j, True, n0, t0)
                    for j in range(4):
                        s5_in_tile(3, j, j < 3, n0, t0)
                    continue
                with pe.Fori(0, rounds) as i:
                    for j in range(4):
                        n = i * 4 + (n0 + j)
                        two = tiles == 2
                        tj = j // 2 if two else j
                        tau = i * tiles + (t0 + tj)
                        for q in range(QUARTERS):
                            if name in norm_of and j == 0:
                                pe.wait_ge(S("act_ready"), 1 + KT * norm_of[name] + QK * (q + 1))
                            if name == "gout" and j == 0 and q == 0:
                                pe.wait_ge(S("mid_lo"), KH)
                            if name[:4] == "down" and j == 0 and q == 0:
                                pe.wait_ge(S("hidden_lo"), 1 + 32 * (2 * int(name[4]) + int(name[5]) + 1))
                            if name == "s5out" and j == 0 and q == 0:
                                pe.wait_ge(S("s5_lo"), 1 + KT)
                            multiply(pe, n, q, j % 2, tj % 2, act if tiles == 4 and name != "s5out" else mid,
                                     k0=KT * (j % 2) if two else 0, kend=2 * KT if two else KT,
                                     tile_free=tau - 1 if q == 0 and (not two or j % 2 == 0) else None)
                        if name[:3] == "ple":
                            l = int(name[3])
                            ct = 4 * i + j
                            pe.wait_ge(S(f"wp_in{j % 2}"), 16 * (8 * l + 1 + j // 2) + 32 * i)
                            if l or j >= 2:
                                pe.wait_ge(S("proj_read"), 1 + 16 * l + 4 * i + j - 1)
                            else:
                                pe.wait_ge(S("proj_read"), 1 + 4 * i)
                            pe.matmul((C, Dk)[j % 2][:, 0:NT], wp[:, j % 2, 0, :], pT[:, 0, :], start=True, stop=False)
                            pe.matmul((C, Dk)[j % 2][:, 0:NT], wp[:, j % 2, 1, :], pT[:, 1, :], start=False,
                                      stop=True).then_inc(S("projected"), 1)
            norm_sums(pe, K_FINAL)
            for g in range(8):
                b, c4 = g // 4, g % 4
                pe.wait_ge(S("final_ready"), KT)
                if g >= 2:
                    pe.wait_ge(S("row_ready"), g - 1)
                for a in range(4):
                    mm = pe.transpose((A, B)[g % 2][:, a * P:(a + 1) * P], h[:, 4 * c4 + a, b * P:(b + 1) * P], ident)
                mm.then_inc(S("row_turned"), 1)

        @block.scalar
        def _(se):
            for name in ("rot_ready",):
                se.sem_inc(S(name), 1)
            link_n = [0]

            def link(ins):
                link_n[0] += 1
                ins.then_inc(S("scalar_setup"), 1)
                se.wait_ge(S("scalar_setup"), link_n[0])
                return ins

            def A_(dst, src, f=ACT.Copy, **kw):
                return se.activation(dst, src, f, **kw)

            for q in range(QUARTERS):
                split_hi(se, 0, q, 0, 1, reused=False, par=0)
            se.wait_ge(S("x_in"), 16)
            for b in range(2):
                mm = A_(h0[:, 8 * b:8 * b + 8, :].rearrange("p k n -> p (k n)"), xn[:, b, :], ACT.Square,
                        accum_out=stat[:, b:b + 1])
                mm.then_inc(S("x_squared"), 1)
            se.wait_ge(S("x_squared"), 2)
            se.wait_ge(S("params_in"), 16 * N_PARAMS)
            A_(stat[:, 2:4], stat[:, 0:2], ACT.Sqrt, scale=1.0 / D, bias=eps[:, 0:1]).then_inc(S("x_squared"), 1)
            se.wait_ge(S("vectors_turned"), 2)
            A_(vec[:, :], A[:, 0:P])
            A_(conv_w[:, :, :].rearrange("p a b -> p (a b)"), A[:, P:3 * P])
            link(A_(cf[:, 0:2, :].rearrange("p a b -> p (a b)"), A[:, 3 * P:4 * P]))
            A_(cf[:, 2, :], B[:, 0:64], ACT.Exp).then_inc(S("vectors_ready"), 2)
            for g in range(8):
                se.wait_ge(S("x_turned"), g + 1)
                se.wait_ge(S("x_squared"), 2)
                A_(h0[:, 2 * g:2 * g + 2, :].rearrange("p k n -> p (k n)"), (C, Dk, E, F)[g % 4][:, :]).then_inc(S("h0_ready"), 1)
            bh = mid[:, 0:2, :].rearrange("p a n -> p (a n)")
            A_(bh, ba_w[:, :]).then_inc(S("ba_hi"), 1)
            se.wait_ge(S("vectors_ready"), 2)
            for kt in range(KT):
                se.wait_ge(S("x_turned"), 8 + kt // 2 + 1)
                A_(act[:, kt, 0:NT], (C, Dk, E, F)[kt // 2 % 4][:, (kt % 2) * NT:(kt % 2 + 1) * NT],
                   scale=vec[:, V_MIX + kt:V_MIX + kt + 1]).then_inc(S("x_hi"), 1)
            se.wait_ge(S("setup_vectors"), 1)
            A_(cf[:, 5, :], cf[:, 4, :], ACT.Exp).then_inc(S("setup_functions"), 1)
            se.wait_ge(S("setup_vectors"), 2)
            A_(cf[:, 11, :], cf[:, 10, :], ACT.Sin)
            A_(cf[:, 12, :], cf[:, 10, :], ACT.Sin, scale=0.5).then_inc(S("setup_functions"), 1)
            se.wait_ge(S("setup_vectors"), 3)
            A_(cf[:, 13, :], cf[:, 13, :], ACT.Sin).then_inc(S("setup_functions"), 1)
            se.wait_ge(S("ba_done"), 1)
            v = A[:, 0:P].rearrange("p (b k h) -> p b k h", b=2, k=2)
            gv = lambda i: ga[:, i, :].rearrange("p (b h) -> p b h", b=2)
            A_(gv(0), v[:, :, 0, :], ACT.Exp, scale=-1.0).then_inc(S("setup_functions"), 1)
            A_(abias[:, 2, :], abias[:, 0, :], ACT.Exp).then_inc(S("setup_functions"), 1)
            se.wait_ge(S("setup_vectors"), 5)
            A_(ga[:, 5, :], ga[:, 4, :], ACT.Exp, scale=-1.0).then_inc(S("setup_functions"), 1)
            se.wait_ge(S("setup_vectors"), 6)
            A_(ga[:, 6, :], ga[:, 5, :], ACT.Ln).then_inc(S("setup_functions"), 1)
            se.wait_ge(S("gc_done"), 1)
            A_(ga[:, 9, :], B[:, 0:64], ACT.Exp)
            A_(ga[:, 1, :], B[:, 128:192], ACT.Exp)
            A_(ga[:, 3, :], B[:, 192:256], ACT.Exp).then_inc(S("setup_functions"), 1)
            se.wait_ge(S("setup_vectors"), 8)
            A_(ga[:, 11, :], ga[:, 11, :], ACT.Exp).then_inc(S("setup_functions"), 1)

            def gate_tanh(n, par, src, ready, v_ready, first=False):
                se.wait_ge(S(ready), v_ready)
                if not first:
                    se.wait_ge(S("gated"), n - 1)
                A_(tanh[:, par, :], src, ACT.Tanh, scale=0.5).then_inc(S("tanh_ready"), 1)

            def front(hd, j, first=False):
                n = 6 * hd + j
                half_copy(se, n + 1, n, j % 2, first=first)
                gate_tanh(n, j % 2, y[:, j, :], "conv_done", 4 * hd + j + 1, first)

            def front_z(r, j):
                n = 6 * r + 4 + j
                half_copy(se, n + 1, n, j)
                gate_tanh(n, j, z[:, j, :], "acc_freed", n + 1)

            for n in range(4):
                for q in range(QUARTERS):
                    split_hi(se, n + 1, q, (n + 1) % 3, (n + 1) // 3 + 1, reused=n + 1 >= 2, par=(n + 1) % 2)
                if n < 3:
                    front(0, n, first=n < 2)

            def core(r, s):
                w = lambda name, k=1, o=1: se.wait_ge(S(name), k * r + o)
                fl = lambda a: a[:, :, :].rearrange("p m q -> p (m q)")
                if s == 0:
                    se.wait_ge(S("gated"), 6 * r + 2)
                    A_(fl(sq), y[:, 0:2, :].rearrange("p a n -> p (a n)"), ACT.Square).then_inc(S("sq_ready"), 1)
                elif s == 1:
                    w("ssum")
                    A_(fl(rn), A[:, :], ACT.Sqrt, scale=0.25, bias=eps[:, 0:1]).then_inc(S("qk_length"), 1)
                    w("gcrow")
                    A_(fl(erow), C[:, :], ACT.Exp).then_inc(S("erow_ready"), 1)
                    w("d1_ready")
                    A_(fl(D1), fl(D1), ACT.Exp, scale=-1.0).then_inc(S("D1_ready"), 1)
                    w("d2_ready")
                    A_(fl(qkT), fl(qkT), ACT.Exp).then_inc(S("D2_ready"), 1)
                elif s == 3:
                    w("PT_turned")
                    A_(fl(PT), A[:, :]).then_inc(S("PT_ready"), 1)
                    w("hs_ready")
                    w("vk_turned")
                    for m in range(4):
                        mm = A_(Vb[:, m, :], Dk[:, m * P:(m + 1) * P], scale=hs[:, H_BHALF + m:H_BHALF + m + 1])
                    mm.then_inc(S("Vb_ready"), 1)
                elif s == 4:
                    w("P2_done")
                    w("L_ready")
                    A_(fl(P2), C[:, :]).then_inc(S("P2_ready"), 1)
                    for m in range(4):
                        mm = A_(Kbe[:, m, :], E[:, (m // 2) * P:(m // 2 + 1) * P], scale=hs[:, H_BEXP + m:H_BEXP + m + 1])
                    mm.then_inc(S("Kbe_ready"), 1)
                elif s == 5:
                    w("P4_done")
                    A_(fl(P4), C[:, :]).then_inc(S("P4_ready"), 1)
                    for m in range(4):
                        mm = A_(kd[:, m, :], E[:, (m // 2) * P:(m // 2 + 1) * P], scale=hs[:, H_KD + m:H_KD + m + 1])
                    mm.then_inc(S("kd_ready"), 1)
                elif s == 6:
                    w("P8_done")
                    A_(fl(P8), C[:, :]).then_inc(S("P8_ready"), 1)
                elif s == 8:
                    w("D1_turned")
                    A_(fl(Dm), C[:, :]).then_inc(S("Dm_ready"), 1)
                elif s == 9:
                    w("W1_done")
                    A_(fl(WT), A[:, :]).then_inc(S("WT_ready"), 1)
                elif s == 11:
                    w("D2_turned")
                    A_(fl(Dm), A[:, :]).then_inc(S("Dm_ready"), 1)
                    w("W2_done")
                    A_(fl(WT), F[:, :]).then_inc(S("WT_ready"), 1)
                elif s == 13:
                    w("W_done")
                    A_(fl(nW), F[:, :], scale=-1.0).then_inc(S("nW_ready"), 1)
                elif s == 20:
                    w("ot_done")
                    A_(fl(osq), B[:, :], ACT.Square).then_inc(S("osq_ready"), 1)
                elif s == 21:
                    w("osum_done")
                    A_(fl(orn), E[:, :], ACT.Sqrt, scale=1.0 / (128 * 128), bias=eps[:, 0:1]).then_inc(S("o_rms"), 1)
                elif s == 22:
                    w("oy_ready")
                    A_(mid[:, ds(2 * r, 2), 0:NT] if not isinstance(r, int) else mid[:, 2 * r:2 * r + 2, 0:NT],
                       oy[:, :, :].rearrange("p (a m) q -> p a (m q)", a=2)).then_inc(S("mid_hi"), 1)

            def head(r, last):
                for s in range(24):
                    if s < 8 or not last:
                        c, q = s // 4, s % 4
                        m = 5 + c
                        if last and c == 1:
                            split_hi(se, GDN_CHUNKS, q, 0, landed_before(GDN_CHUNKS), par=0)
                        else:
                            split_hi(se, 6 * r + m, q, m % 3, 2 * r + m // 3 + 1, par=m % 2)
                    if s == 0:
                        front(r, 3)
                    if s in (4, 8):
                        front_z(r, s // 4 - 1)
                    if s in (12, 16, 20) and not last:
                        front(r + 1, s // 4 - 3)
                    core(r, s)

            with se.Fori(0, KH - 1) as r:
                head(r, False)
            head(KH - 1, True)

            def next_hi(i, name, j, nxt_first):
                n0 = plan[name][0]
                s = (j + 1) % 4
                landed = i + (landed_before(n0 + j + 1))
                return n0 + j + 1, s, landed

            def splits(i, name, j):
                n0, t0, rounds, chunks, tiles = plan[name]
                s = (j + 1) % 4
                n = i * 4 + (n0 + j + 1)
                for q in range(QUARTERS):
                    split_hi(se, n, q, s, i + landed_before(n0 + j + 1), par=(j + 1) % 2)

            def tile_post(name, i, j, tj):
                n0, t0, rounds, chunks, tiles = plan[name]
                tau = i * tiles + (t0 + tj)
                half_copy(se, i * 4 + (n0 + j + 1), tau, tj % 2)
                if name[:2] == "up":
                    tile = 32 * (2 * int(name[2]) + int(name[3]))
                    se.wait_ge(S("hidden"), i * 4 + (tile + j + 1))
                    A_(mid[:, ds(i * 4 + j, 1), 0:NT], normed[:, j % 2, :]).then_inc(S("hidden_hi"), 1)
                elif name[:3] == "ple":
                    se.wait_ge(S("acc_freed"), tau + 1)
                    A_(tanh[:, j % 2, :], summed[:, j % 2, :], ACT.Tanh, scale=0.5).then_inc(S("gate_tanh"), 1)
                elif name == "s5out" and j % 2:
                    se.wait_ge(S("acc_freed"), tau + 1)
                    A_(tanh[:, 1, :], summed[:, 1, :], ACT.Tanh, scale=0.5).then_inc(S("glu_tanh"), 1)

            def s5_tile(i, j, more):
                n0, t0 = plan["s5in"][0:2]
                ct = 4 * i + j
                se.wait_ge(S("bc_turned"), 1 + ct + 1)
                A_(bcT[:, :, :].rearrange("p a q -> p (a q)"), B[:, :]).then_inc(S("bcT_ready"), 1)
                for r4 in range(4):
                    se.wait_ge(S("turns_ready"), 1 + 4 * ct + r4 + 1)
                    if r4 < 2 and not isinstance(i, int) and j == 0:
                        se.wait_ge(S("x2_ready"), 1 + 16 * i)
                    elif isinstance(i, int) or j or r4 >= 2:
                        se.wait_ge(S("x2_ready"), 1 + 4 * ct + r4 - 1)
                    a = r4 % 2
                    A_(rot[:, a, 0, :], turn[:, a, 1, :], ACT.Sin, scale=TWO_PI)
                    A_(rot[:, a, 1, :], turn[:, a, 0, :], ACT.Sin, scale=-TWO_PI)
                    A_(rot[:, a, 2, :], turn[:, a, 0, :], ACT.Sin, scale=TWO_PI)
                    A_(rot[:, a, 3, :], turn[:, a, 0, :], ACT.Sin, scale=-TWO_PI).then_inc(S("rot_ready"), 1)
                    if more:
                        split_hi(se, n0 + ct + 2 if not more == 2 else n0 + ct + 2, r4, (j + 2) % 4,
                                 i + landed_before(n0 + j + 2), par=j % 2)
                if isinstance(i, int) is False or j < 3:
                    half_copy(se, n0 + ct + 2, t0 + ct + 1, (j + 1) % 2)
                se.wait_ge(S("gelu_in"), 1 + ct + 1)
                A_(gl[:, 1, :], gl[:, 0, :], ACT.Square).then_inc(S("gelu_sq"), 1)
                se.wait_ge(S("gelu_arg"), ct + 1)
                A_(gl[:, 1, :], gl[:, 1, :], ACT.Tanh, scale=math.sqrt(2 / math.pi)).then_inc(S("gelu_tanh"), 1)
                se.wait_ge(S("gelu_ready"), ct + 1)
                A_(mid[:, ds(ct, 1), 0:NT] if not isinstance(i, int) else mid[:, ct:ct + 1, 0:NT], gl[:, 0, :],
                   scale=0.5).then_inc(S("s5_hi"), 1)

            for name, (n0, t0, rounds, chunks, tiles) in plan.items():
                last_phase = name == list(plan)[-1]
                if name in norm_of:
                    k = norm_of[name]
                    norm_squares(se, k, h_done[name])
                    norm_apply_scalar(se, k)
                if name[:3] == "ple":
                    l = int(name[3])
                    se.wait_ge(S("p_turned"), l + 1)
                    A_(pT[:, :, :].rearrange("p e n -> p (e n)"), E[:, :]).then_inc(S("pT_ready"), 1)
                if name == "s5in":
                    for q in range(QUARTERS):
                        split_hi(se, n0 + 1, q, 1, landed_before(n0 + 1), par=1)
                    half_copy(se, n0 + 1, t0, 0)
                    with se.Fori(0, 3) as i:
                        for j in range(4):
                            s5_tile(i, j, 1)
                    for j in range(4):
                        s5_tile(3, j, 1 if j < 3 else 0)
                    continue
                full = rounds - 1 if last_phase else rounds
                with se.Fori(0, full) as i:
                    for j in range(4):
                        splits(i, name, j)
                        if tiles == 4 or j % 2:
                            tile_post(name, i, j, j if tiles == 4 else j // 2)
                if last_phase:
                    i = rounds - 1
                    for j in range(4):
                        if j < 3:
                            splits(i, name, j)
                        if tiles == 4 or j % 2:
                            tile_post(name, i, j, j if tiles == 4 else j // 2)
            norm_squares(se, K_FINAL, H_FINAL)
            for g in range(8):
                se.wait_ge(S("row_turned"), g + 1)
                if g >= 2:
                    se.wait_ge(S(f"stored{g % 2}"), 16 * (g // 2))
                A_(row_out[:, g % 2, :], (A, B)[g % 2][:, :]).then_inc(S("row_ready"), 1)

        @block.gpsimd
        def _(gp):
            if "s5in" not in plan:
                return
            for name in ("turns_ready",):
                gp.sem_inc(S(name), 1)
            gp.wait_ge(S("t_in"), 16)
            gp.wait_ge(S("sq_summed"), 1 + KT * (norm_of["s5in"] + 1))
            gp.memset(b_blk[:, :, :, :, :].rearrange("p a r g e -> p (a r g e)"), 0.0).then_inc(S("blk_zero"), 1)
            gp.wait_ge(S("blk_zero"), 1)
            gp.wait_ge(S("setup_vectors"), 4)

            def spread(i, j):
                ct = i * 4 + j
                a = j % 2
                gp.wait_ge(S(f"bc_in{a}"), i * 128 + 64 * (j // 2 + 1))
                q4 = ds(i * 16 + 4 * j, 4) if not isinstance(i, int) else slice(16 * i + 4 * j, 16 * i + 4 * j + 4)
                co = [s5v[:, 3 + e, q4].unsqueeze(2).to_broadcast([P, 4, 16]) for e in range(2)]
                for e, (x, y_) in enumerate(((0, 0), (1, 1), (0, 1), (1, 0))):
                    mm = gp.tensor_tensor(b_t[:, e, :].rearrange("p (r e) -> p r e", r=4), b_in[:, a, x, :, :], co[y_], ALU.mult)
                mm.then_inc(S("b_products"), 1)
                gp.wait_ge(S("b_products"), ct + 1)
                gp.wait_ge(S("bc_turned"), 1 + ct)
                for g in range(2):
                    rws = slice(64 * g, 64 * g + 64)
                    bt = lambda e: b_t[rws, e, :].rearrange("p (r e) -> p r e", r=4)
                    gp.tensor_tensor(b_blk[rws, 0, :, g, :], bt(0), bt(1), ALU.subtract)
                    gp.tensor_tensor(b_blk[rws, 1, :, g, :], bt(2), bt(3), ALU.add).then_inc(S("blk_half"), 1)
                    gp.wait_ge(S("blk_half"), ct * 2 + g + 1)
                for e in range(2):
                    mm = gp.tensor_tensor(c_blk[:, e, :, :], c_in[:, a, e, :].unsqueeze(1).to_broadcast([P, 2, 64]),
                                          tcol[:, NT + 2 * e:NT + 2 * e + 2].unsqueeze(2).to_broadcast([P, 2, 64]), ALU.mult)
                mm.then_inc(S("spread"), 1)

            def turns(i, j, r4):
                pi = i * 16 + (4 * j + r4)
                a = r4 % 2
                tf = tcol[:, 0:NT]
                at = ds(pi, 1) if not isinstance(pi, int) else slice(pi, pi + 1)
                gp.wait_ge(S("turns_ready"), 1 + pi)
                gp.tensor_copy(tq[:, :, :], s5v[:, 1:3, at]).then_inc(S("turn_step"), 1)
                if isinstance(i, int) or j or r4 >= 2:
                    gp.wait_ge(S("rot_ready"), 1 + pi - 1)
                else:
                    gp.wait_ge(S("rot_ready"), 1 + i * 16)
                big, quarter = tcol[:, NT + 4:NT + 5], tcol[:, NT + 5:NT + 6]
                done = [1]

                def after():
                    gp.wait_ge(S("turn_step"), pi * 9 + done[0])
                    done[0] += 1

                after()
                gp.tensor_tensor(turn[:, a, 0, :], tf, tq[:, 0, :].to_broadcast([P, NT]), ALU.mult)
                gp.tensor_tensor(tw[:, 1, :], tf, tq[:, 1, :].to_broadcast([P, NT]), ALU.mult).then_inc(S("turn_step"), 1)
                after()
                gp.tensor_tensor(tw[:, 0, :], turn[:, a, 0, :], big.to_broadcast([P, NT]), ALU.add).then_inc(S("turn_step"), 1)
                after()
                gp.tensor_tensor(tw[:, 0, :], tw[:, 0, :], big.to_broadcast([P, NT]), ALU.subtract).then_inc(S("turn_step"), 1)
                after()
                gp.tensor_tensor(turn[:, a, 0, :], turn[:, a, 0, :], tw[:, 0, :], ALU.subtract).then_inc(S("turn_step"), 1)
                after()
                gp.tensor_tensor(turn[:, a, 0, :], turn[:, a, 0, :], tw[:, 1, :], ALU.add).then_inc(S("turn_step"), 1)
                after()
                gp.tensor_tensor(turn[:, a, 1, :], turn[:, a, 0, :], quarter.to_broadcast([P, NT]), ALU.add).then_inc(S("turn_step"), 1)
                after()
                bigs = big.unsqueeze(1).to_broadcast([P, 2, NT])
                gp.tensor_tensor(tw[:, :, :], turn[:, a, :, :], bigs, ALU.add).then_inc(S("turn_step"), 1)
                after()
                gp.tensor_tensor(tw[:, :, :], tw[:, :, :], bigs, ALU.subtract).then_inc(S("turn_step"), 1)
                after()
                gp.tensor_tensor(turn[:, a, :, :], turn[:, a, :, :], tw[:, :, :], ALU.subtract).then_inc(S("turns_ready"), 1)

            spread(0, 0)
            with gp.Fori(0, 3) as i:
                for j in range(4):
                    for r4 in range(4):
                        turns(i, j, r4)
                    spread(i, j + 1)
            for j in range(4):
                for r4 in range(4):
                    turns(3, j, r4)
                if j < 3:
                    spread(3, j + 1)

        @block.vector
        def _(ve):
            for name in ("x2_ready", "s5_lo", "gelu_in", "glu_ready", "act_ready", "h_updated", "proj_read", "hidden_lo"):
                ve.sem_inc(S(name), 1)
            link_n = [0]

            def link(ins):
                link_n[0] += 1
                ins.then_inc(S("vector_setup"), 1)
                ve.wait_ge(S("vector_setup"), link_n[0])

            TT, TS, STT = ve.tensor_tensor, ve.tensor_scalar, ve.scalar_tensor_tensor
            ve.wait_ge(S("params_in"), 16 * N_PARAMS)
            ve.tensor_copy(rows[0:64, 4, :].rearrange("p (g q) -> p g q", g=2),
                           ls2[0:64, :].unsqueeze(2).to_broadcast([64, 2, 64])).then_inc(S("steps_ready"), 1)
            for q in range(QUARTERS):
                split_lo(ve, 0, q, 0, 0)
            ve.wait_ge(S("x_squared"), 3)
            link(ve.reciprocal(stat[:, 4:6], stat[:, 2:4]))
            ve.wait_ge(S("x_turned"), 8)
            for b in range(2):
                TS(xn[:, b, :], xn[:, b, :], stat[:, 4 + b:5 + b], None, ALU.mult).then_inc(S("x_scaled"), 1)
            ve.wait_ge(S("ba_hi"), 1)
            TT(mid[:, 2:4, :].rearrange("p a n -> p (a n)"), ba_w[:, :],
               mid[:, 0:2, :].rearrange("p a n -> p (a n)").bitcast(F32), ALU.subtract).then_inc(S("ba_lo"), 1)
            for kt in range(KT):
                ve.wait_ge(S("x_hi"), 2 * (kt // 2) + 2)
                STT(act[:, kt, NT:2 * NT], (C, Dk, E, F)[kt // 2 % 4][:, (kt % 2) * NT:(kt % 2 + 1) * NT],
                    vec[:, V_MIX + kt:V_MIX + kt + 1], act[:, kt, 0:NT].bitcast(F32), ALU.mult,
                    ALU.subtract).then_inc(S("act_ready0"), 1)

            c_ = lambda i: cf[:, i, :]
            s_ = lambda i: s5v[:, i, :]
            ve.wait_ge(S("vectors_ready"), 2)
            TT(c_(4), c_(0), c_(2), ALU.mult).then_inc(S("setup_vectors"), 1)
            link(TT(c_(3), c_(1), c_(2), ALU.mult))
            link(TS(c_(8), c_(3), 1 / TWO_PI_EXACT, MAGIC, ALU.mult, ALU.add))
            link(TS(c_(8), c_(8), MAGIC, None, ALU.subtract))
            link(STT(c_(10), c_(8), -TP1, c_(3), ALU.mult, ALU.add))
            link(STT(c_(10), c_(8), -TP2, c_(10), ALU.mult, ALU.add))
            link(STT(c_(10), c_(8), -TP3, c_(10), ALU.mult, ALU.add))
            TS(c_(10), c_(10), PI_BELOW, -PI_BELOW, ALU.min, ALU.max).then_inc(S("setup_vectors"), 1)
            ve.wait_ge(S("setup_vectors"), 2)
            link(TS(c_(14), c_(10), 1 / TWO_PI_EXACT, 4096.0, ALU.mult, ALU.mult))
            link(TS(c_(14), c_(14), MAGIC, MAGIC, ALU.add, ALU.subtract))
            link(TS(s_(1), c_(14), 1 / 4096.0, None, ALU.mult))
            link(STT(c_(14), s_(1), -TP1, c_(10), ALU.mult, ALU.add))
            link(STT(c_(14), s_(1), -TP2, c_(14), ALU.mult, ALU.add))
            link(STT(c_(14), s_(1), -TP3, c_(14), ALU.mult, ALU.add))
            link(TS(s_(2), c_(14), 1 / TWO_PI_EXACT, None, ALU.mult))
            link(STT(c_(13), c_(10), -1.0, c_(10), ALU.mult, ALU.min))
            TS(c_(13), c_(13), math.pi / 2, None, ALU.add).then_inc(S("setup_vectors"), 1)
            link(TS(c_(6), c_(4), -1.0, 1.0, ALU.max, ALU.min))
            link(TS(c_(6), c_(6), 0.25, None, ALU.mult))
            link(TS(c_(7), c_(6), 1 / 8.0, 1.0, ALU.mult, ALU.add))
            for d in (7, 6, 5, 4, 3, 2):
                link(TT(c_(7), c_(7), c_(6), ALU.mult))
                link(TS(c_(7), c_(7), 1.0 / d, 1.0, ALU.mult, ALU.add))
            link(TT(c_(7), c_(7), c_(6), ALU.mult))
            for _ in range(2):
                link(STT(c_(7), c_(7), 2.0, c_(7), ALU.add, ALU.mult))
            ve.wait_ge(S("setup_functions"), 1)
            link(TS(c_(5), c_(5), 1.0, None, ALU.subtract))
            link(STT(c_(8), c_(4), -1.0, c_(4), ALU.mult, ALU.max))
            link(TS(c_(8), c_(8), 1.0, None, ALU.is_lt))
            link(TT(c_(7), c_(7), c_(5), ALU.subtract))
            link(TT(c_(7), c_(7), c_(8), ALU.mult))
            link(TT(c_(7), c_(7), c_(5), ALU.add))
            link(TS(s_(0), c_(7), 1.0, None, ALU.add))
            ve.wait_ge(S("setup_functions"), 2)
            ve.wait_ge(S("setup_functions"), 3)
            link(TT(c_(12), c_(12), c_(12), ALU.mult))
            link(TT(c_(13), c_(13), c_(7), ALU.mult))
            link(STT(c_(12), c_(12), -2.0, c_(13), ALU.mult, ALU.add))
            link(TT(c_(11), c_(11), s_(0), ALU.mult))
            link(TT(c_(5), c_(0), c_(0), ALU.mult))
            link(TT(c_(6), c_(1), c_(1), ALU.mult))
            link(TT(c_(5), c_(5), c_(6), ALU.add))
            link(ve.reciprocal(c_(5), c_(5)))
            link(TT(c_(6), c_(12), c_(0), ALU.mult))
            link(TT(c_(8), c_(11), c_(1), ALU.mult))
            link(TT(c_(6), c_(6), c_(8), ALU.add))
            link(TT(s_(3), c_(6), c_(5), ALU.mult))
            link(TT(c_(6), c_(11), c_(0), ALU.mult))
            link(TT(c_(8), c_(12), c_(1), ALU.mult))
            link(TT(c_(6), c_(6), c_(8), ALU.subtract))
            TT(s_(4), c_(6), c_(5), ALU.mult).then_inc(S("setup_vectors"), 1)

            gv = lambda i: ga[:, i, :].rearrange("p (b h) -> p b h", b=2)
            ve.wait_ge(S("setup_functions"), 4)
            link(TS(ga[:, 1, :], ga[:, 0, :], 1.0, None, ALU.add))
            link(ve.reciprocal(ga[:, 2, :], ga[:, 1, :]))
            v = A[:, 0:P].rearrange("p (b k h) -> p b k h", b=2, k=2)
            link(TT(gv(3), v[:, :, 1, :], abias[:, 1, :].unsqueeze(1).to_broadcast([P, 2, 32]), ALU.add))
            STT(ga[:, 4, :], ga[:, 3, :], -1.0, ga[:, 3, :], ALU.mult, ALU.max).then_inc(S("setup_vectors"), 1)
            ve.wait_ge(S("setup_functions"), 6)
            TS(ga[:, 5, :], ga[:, 5, :], 1.0, None, ALU.add).then_inc(S("setup_vectors"), 1)
            ve.wait_ge(S("setup_functions"), 7)
            link(STT(ga[:, 7, :], ga[:, 3, :], 0.0, ga[:, 6, :], ALU.max, ALU.add))
            ve.wait_ge(S("setup_functions"), 5)
            STT(gv(8), gv(7), -1.0, abias[:, 2, :].unsqueeze(1).to_broadcast([P, 2, 32]), ALU.mult,
                ALU.mult).then_inc(S("setup_vectors"), 1)
            ve.wait_ge(S("setup_functions"), 8)
            link(ve.tensor_copy(ga[:, 0, :], B[:, 0:64]))
            TT(ga[:, 11, :], B[:, 64:128], ga[:, 0, :], ALU.subtract).then_inc(S("setup_vectors"), 1)
            ve.wait_ge(S("setup_functions"), 8)
            TT(ga[:, 10, :], ga[:, 2, :], ga[:, 9, :], ALU.mult)
            link(TS(ga[:, 4, :], ga[:, 2, :], 0.5, None, ALU.mult))
            ve.wait_ge(S("setup_functions"), 9)
            ve.wait_ge(S("setup_vectors"), 7)
            for b in range(2):
                for col, i in ((H_BETA, 2), (H_GC, 0), (H_BEXP, 10), (H_KD, 11), (H_G, 8), (H_BHALF, 4)):
                    ve.tensor_copy(gt[:, :, col + 2 * b:col + 2 * b + 2],
                                   ga[:, i, 32 * b:32 * b + 32].rearrange("p (i h) -> p i h", h=2))
                for hc in range(2):
                    last = ve.tensor_copy(gt[:, :, H_GLAST + 4 * b + 2 * hc:H_GLAST + 4 * b + 2 * hc + 2],
                                          ga[:, (1, 3)[hc], 32 * b:32 * b + 32].rearrange("p (i h) -> p i h", h=2))
            link(last)
            link(ve.memset(pre[:, :, 0:4], 0.0))
            link(TS(onorm[:, :], onorm[:, :], 0.5 * 128 ** -0.5, None, ALU.mult))
            ve.wait_ge(S("h_saved"), 16)

            def gate(n, par, dst):
                ve.wait_ge(S("tanh_ready"), n + 1)
                STT(dst, tanh[:, par, :], 1.0, dst, ALU.add, ALU.mult).then_inc(S("gated"), 1)

            def front(hd, j):
                n, fi = 6 * hd + j, 4 * hd + j
                sum_halves(ve, n, j % 2, pre[:, j, 3:NT + 3])
                tile = (hd, hd + 16, 2 * hd + 32, 2 * hd + 33)[j]
                at = ds(tile, 1) if not isinstance(tile, int) else slice(tile, tile + 1)
                ve.tensor_copy(conv_f[:, j, :].unsqueeze(2), conv_w[:, :, at]).then_inc(S("taps_ready"), 1)
                ve.wait_ge(S("acc_freed"), n + 1)
                ve.wait_ge(S("taps_ready"), fi + 1)
                TS(y[:, j, :], pre[:, j, 0:NT], conv_f[:, j, 0:1], None, ALU.mult).then_inc(S("tap_added"), 1)
                for k in range(1, 4):
                    ve.wait_ge(S("tap_added"), 3 * fi + k)
                    ins = STT(y[:, j, :], pre[:, j, k:k + NT], conv_f[:, j, k:k + 1], y[:, j, :], ALU.mult, ALU.add)
                    ins.then_inc(S("tap_added" if k < 3 else "conv_done"), 1)
                gate(n, j % 2, y[:, j, :])

            def front_z(r, j):
                n = 6 * r + 4 + j
                sum_halves(ve, n, j, z[:, j, :])
                gate(n, j, z[:, j, :])

            for n in range(4):
                for q in range(QUARTERS):
                    split_lo(ve, n + 1, q, (n + 1) % 3, (n + 1) % 2)
                if n < 3:
                    front(0, n)

            def core(r, s):
                w = lambda name, k=1, o=1: ve.wait_ge(S(name), k * r + o)
                fl = lambda a: a[:, :, :].rearrange("p m q -> p (m q)")
                hcol = lambda c: hs[:, c:c + 1]
                bh = lambda a: a[:, :, :].rearrange("p (b h) q -> p b h q", b=2)
                if s == 0:
                    at = ds(r, 1) if not isinstance(r, int) else slice(r, r + 1)
                    ve.tensor_copy(hs[:, :].unsqueeze(1), gt[:, at, :]).then_inc(S("hs_ready"), 1)
                elif s == 1:
                    w("qk_length")
                    ve.reciprocal(fl(rn), fl(rn)).then_inc(S("qk_inverse"), 1)
                    w("qk_inverse")
                    ve.wait_ge(S("gated"), 6 * r + 2)
                    STT(fl(qkn), y[:, 0:2, :].rearrange("p a n -> p (a n)"), 0.5, fl(rn), ALU.mult,
                        ALU.mult).then_inc(S("qkn_ready"), 1)
                    w("gcrow")
                    w("erow_ready")
                    w("hs_ready")
                    for m in range(4):
                        last = TS(D1[:, m, :], C[:, m * P:(m + 1) * P], hcol(H_GC + m), 0.0, ALU.subtract, ALU.max)
                    last.then_inc(S("d1_ready"), 1)
                    for m in range(4):
                        last = TS(qkT[:, m, :], C[:, m * P:(m + 1) * P], hcol(H_GC + m), 0.0, ALU.subtract, ALU.min)
                    last.then_inc(S("d2_ready"), 1)
                elif s == 2:
                    w("attn_done")
                    w("D1_ready")
                    for m in range(4):
                        b = m // 2
                        last = STT(Mp[:, m, :], B[:, b * NT + P:b * NT + 2 * P], hcol(H_BETA + m), D1[:, m, :],
                                   ALU.mult, ALU.mult)
                    last.then_inc(S("M_ready"), 1)
                    w("M_ready")
                    mk = lambda k: masks[:, k, :].unsqueeze(1).to_broadcast([P, 4, P])
                    TT(Pm[:, :, :], Mp[:, :, :], mk(2), ALU.mult).then_inc(S("P_ready"), 1)
                    TT(L1[:, :, :], Mp[:, :, :], mk(3), ALU.mult)
                    TT(L2[:, :, :], Mp[:, :, :], mk(4), ALU.mult).then_inc(S("L_ready"), 1)
                elif s == 3:
                    w("PT_ready")
                    TT(RT[:, :, :], PT[:, :, :],
                       ident.unsqueeze(1).to_broadcast([P, 4, P]), ALU.add).then_inc(S("RT_ready"), 1)
                    w("D2_ready")
                    qk = B[:, :].rearrange("p (b a q) -> p b a q", b=2, a=2)[:, :, 0:1, :].to_broadcast([P, 2, 2, P])
                    TT(bh(qkT), bh(qkT), qk, ALU.mult).then_inc(S("qk_decay"), 1)
                    w("qk_decay")
                    TT(qkT[:, :, :], qkT[:, :, :], U.unsqueeze(1).to_broadcast([P, 4, P]), ALU.mult).then_inc(S("qkT_ready"), 1)
                    w("erow_ready")
                    w("qkn_ready")
                    qn = qkn[:, 0:2, :].unsqueeze(2).to_broadcast([P, 2, 2, P])
                    TT(bh(qeT), qn, bh(erow), ALU.mult).then_inc(S("qeT_ready"), 1)
                elif s == 4:
                    w("P2T_done")
                    w("qeT_ready")
                    ve.tensor_copy(fl(P2T), F[:, :]).then_inc(S("P2T_ready"), 1)
                elif s in (5, 6, 7):
                    i = s - 4
                    w("R_done", 5, i)
                    w("RT_ready", 6, i)
                    TT(fl(RT), A[:, :], fl(RT), ALU.add).then_inc(S("RT_ready"), 1)
                    if s == 5:
                        w("P4T_done")
                        ve.tensor_copy(fl(P4T), F[:, :]).then_inc(S("P4T_ready"), 1)
                elif s in (10, 12):
                    i = 4 if s == 10 else 5
                    w("R_done", 5, i)
                    w("RT_ready", 6, i)
                    TT(fl(RT), fl(RT), C[:, :], ALU.subtract).then_inc(S("RT_ready"), 1)
                elif s == 13:
                    w("U_done")
                    ve.tensor_copy(fl(VN), A[:, :]).then_inc(S("VN_ready"), 1)
                elif s == 14:
                    ve.wait_ge(S("kv_done"), 3 * r + 1)
                    ve.tensor_copy(fl(state), C[:, 0:2 * P]).then_inc(S("state_ready"), 1)
                elif s in (15, 17, 19):
                    c = (s - 13) // 2
                    b, lo = c // 2, 64 * (c % 2)
                    ve.wait_ge(S("ws_done"), 3 * r + c)
                    w("VN_ready")
                    dst = VN[lo:lo + 64, 2 * b:2 * b + 2, :].rearrange("p m q -> p (m q)")
                    TT(dst, dst, A[lo:lo + 64, 0:2 * P], ALU.add).then_inc(S("vn_ready"), 1)
                elif s in (16, 18):
                    c = (s - 14) // 2
                    ve.wait_ge(S("kv_done"), 3 * r + c + 1)
                    ve.wait_ge(S("state_ready"), 3 * r + c)
                    for hd in range(2):
                        last = STT(state[:, hd, :], state[:, hd, :], hcol(H_GLAST + 2 * c + hd), C[:, hd * P:(hd + 1) * P],
                                   ALU.mult, ALU.add)
                    last.then_inc(S("state_ready"), 1)
                elif s == 21:
                    w("o_rms")
                    ve.reciprocal(fl(orn), fl(orn)).then_inc(S("o_inverse"), 1)
                elif s == 22:
                    w("o_inverse")
                    TT(fl(oy), B[:, :], fl(orn), ALU.mult).then_inc(S("o_normed"), 1)
                    w("o_normed")
                    ve.wait_ge(S("gated"), 6 * r + 6)
                    STT(fl(oy), fl(oy), onorm[:, 0:1], z[:, :, :].rearrange("p a n -> p (a n)"), ALU.mult,
                        ALU.mult).then_inc(S("oy_ready"), 1)
                    w("oy_ready")
                    w("mid_hi")
                    at = ds(2 * r, 2) if not isinstance(r, int) else slice(2 * r, 2 * r + 2)
                    TT(mid[:, at, NT:2 * NT], oy[:, :, :].rearrange("p (a m) q -> p a (m q)", a=2),
                       mid[:, at, 0:NT].bitcast(F32), ALU.subtract).then_inc(S("mid_lo"), 1)

            def head(r, last):
                for s in range(24):
                    if s < 8 or not last:
                        m = 5 + s // 4
                        split_lo(ve, 6 * r + m, s % 4, 0 if last and m == 6 else m % 3, m % 2)
                    if s == 0:
                        front(r, 3)
                    if s in (4, 8):
                        front_z(r, s // 4 - 1)
                    if s in (12, 16, 20) and not last:
                        front(r + 1, s // 4 - 3)
                    core(r, s)

            with ve.Fori(0, KH - 1) as r:
                head(r, False)
            head(KH - 1, True)

            def tile_post(name, i, j, tj):
                n0, t0, rounds, chunks, tiles = plan[name]
                tau = i * tiles + (t0 + tj)
                a = tj % 2
                if name[:2] == "up":
                    tile = 32 * (2 * int(name[2]) + int(name[3])) + j + 1
                    sum_halves(ve, tau, a, summed[:, a, :])
                    ve.wait_ge(S("acc_freed"), tau + 1)
                    ve.wait_ge(S("hidden_lo"), i * 4 + max(tile - 1, 1))
                    STT(normed[:, a, :], summed[:, a, :], 0.0, summed[:, a, :], ALU.max, ALU.mult).then_inc(S("hidden"), 1)
                    ve.wait_ge(S("hidden_hi"), i * 4 + tile)
                    TT(mid[:, ds(i * 4 + j, 1), NT:2 * NT], normed[:, a, :],
                       mid[:, ds(i * 4 + j, 1), 0:NT].bitcast(F32), ALU.subtract).then_inc(S("hidden_lo"), 1)
                elif name[:3] == "ple":
                    sum_halves(ve, tau, a, summed[:, a, :])
                    ct = i * 4 + (16 * int(name[3]) + j)
                    ve.wait_ge(S("projected"), ct + 1)
                    ve.wait_ge(S("h_updated"), 1 + i * 4 + (h_done[name] + j))
                    ve.wait_ge(S("gate_tanh"), ct + 1)
                    STT(normed[:, a, :], tanh[:, a, :], 1.0, (C, Dk)[a][:, 0:NT], ALU.add, ALU.mult).then_inc(S("proj_read"), 1)
                    ve.wait_ge(S("proj_read"), 1 + ct + 1)
                    hv = h[:, ds(i * 4 + j, 1), :]
                    STT(hv, normed[:, a, :], 0.5, hv, ALU.mult, ALU.add).then_inc(S("h_updated"), 1)
                elif name == "s5out":
                    if not a:
                        ve.wait_ge(S("glu_ready"), 1 + i * 2 + j // 2)
                    sum_halves(ve, tau, a, summed[:, a, :])
                    if a:
                        pair = i * 2 + j // 2
                        ve.wait_ge(S("glu_tanh"), pair + 1)
                        ve.wait_ge(S("h_updated"), 1 + i * 2 + (h_done[name] + j // 2))
                        STT(normed[:, 0, :], tanh[:, 1, :], 1.0, summed[:, 0, :], ALU.add, ALU.mult).then_inc(S("glu_ready"), 1)
                        ve.wait_ge(S("glu_ready"), 1 + pair + 1)
                        hv = h[:, ds(i * 2 + j // 2, 1), :]
                        STT(hv, normed[:, 0, :], 0.5, hv, ALU.mult, ALU.add).then_inc(S("h_updated"), 1)
                else:
                    ve.wait_ge(S("h_updated"), 1 + i * 2 + (h_done[name] + tj))
                    sum_halves(ve, tau, a, summed[:, a, :])
                    ve.wait_ge(S("acc_freed"), tau + 1)
                    hv = h[:, ds(i * 2 + tj, 1), :]
                    TT(hv, hv, summed[:, a, :], ALU.add).then_inc(S("h_updated"), 1)

            def s5_tile(i, j, more):
                n0, t0 = plan["s5in"][0:2]
                ct = i * 4 + j
                at = (lambda x: ds(x, 1)) if not isinstance(i, int) else (lambda x: slice(x, x + 1))
                for r4 in range(4):
                    pi = i * 16 + (4 * j + r4)
                    if more:
                        split_lo(ve, n0 + ct + 2, r4, (j + 2) % 4, j % 2)
                    bk = (C, Dk, E, F)[r4]
                    X = bk[:, :].rearrange("p (a n) -> p a n", a=2)
                    a = r4 % 2
                    cosb = rot[:, a, 0:1, :].to_broadcast([P, 2, NT])
                    ve.wait_ge(S("rot_ready"), 1 + pi + 1)
                    ve.wait_ge(S("bu_done"), pi + 1)
                    ve.wait_ge(S("x2_ready"), 1 + pi)
                    TT(st[:, :, :], X, cosb, ALU.mult)
                    TT(rb[:, :, :], X, rot[:, a, 1:3, :], ALU.mult).then_inc(S("bu_products"), 1)
                    ve.wait_ge(S("bu_products"), pi + 1)
                    TT(st[:, 0, :], st[:, 0, :], rb[:, 1, :], ALU.add)
                    TT(st[:, 1, :], st[:, 1, :], rb[:, 0, :], ALU.add).then_inc(S("bu_turned"), 1)
                    ve.wait_ge(S("bu_turned"), pi + 1)
                    decay = s5v[:, 0, at(pi)].to_broadcast([P, NT])
                    for e in range(2):
                        last = ve.tensor_tensor_scan(st[:, e, :], decay, st[:, e, :], 0.0, ALU.mult, ALU.add)
                    last.then_inc(S("scanned"), 1)
                    ve.wait_ge(S("scanned"), pi + 1)
                    if not (isinstance(pi, int) and pi == 0):
                        ve.wait_ge(S("x1_used"), 1 + pi)
                    TT(x1[:, :, :], st[:, :, :], cosb, ALU.mult).then_inc(S("x1_ready"), 1)
                    ve.wait_ge(S("y_done"), 1 + pi)
                    TT(x2[:, :, :], st[:, :, :], rot[:, a, 2:4, :], ALU.mult).then_inc(S("x2_ready"), 1)
                if not isinstance(i, int) or j < 3:
                    ve.wait_ge(S("gelu_in"), 1 + ct)
                    sum_halves(ve, t0 + ct + 1, (j + 1) % 2, u[:, (j + 1) % 2, :])
                    ve.wait_ge(S("acc_freed"), t0 + ct + 2)
                ve.wait_ge(S("y_done"), 1 + i * 16 + 4 * (j + 1))
                ve.wait_ge(S("s5_lo"), 1 + ct)
                STT(gl[:, 0, :], u[:, j % 2, :], vec[:, ds(i * 4 + (V_D + j), 1)] if not isinstance(i, int)
                    else vec[:, V_D + ct:V_D + ct + 1], A[:, 0:NT], ALU.mult, ALU.add).then_inc(S("gelu_in"), 1)
                ve.wait_ge(S("gelu_sq"), ct + 1)
                TS(gl[:, 1, :], gl[:, 1, :], 0.044715, 1.0, ALU.mult, ALU.add).then_inc(S("gelu_poly"), 1)
                ve.wait_ge(S("gelu_poly"), ct + 1)
                TT(gl[:, 1, :], gl[:, 1, :], gl[:, 0, :], ALU.mult).then_inc(S("gelu_arg"), 1)
                ve.wait_ge(S("gelu_tanh"), ct + 1)
                STT(gl[:, 0, :], gl[:, 1, :], 1.0, gl[:, 0, :], ALU.add, ALU.mult).then_inc(S("gelu_ready"), 1)
                ve.wait_ge(S("s5_hi"), ct + 1)
                STT(mid[:, at(ct), NT:2 * NT], gl[:, 0:1, :], 0.5, mid[:, at(ct), 0:NT].bitcast(F32), ALU.mult,
                    ALU.subtract).then_inc(S("s5_lo"), 1)

            def splits(i, name, j):
                n0 = plan[name][0]
                for q in range(QUARTERS):
                    split_lo(ve, i * 4 + (n0 + j + 1), q, (j + 1) % 4, (j + 1) % 2)

            for name, (n0, t0, rounds, chunks, tiles) in plan.items():
                last_phase = name == list(plan)[-1]
                if name == "gout":
                    ve.wait_ge(S("h_loaded"), 16)
                elif h_done[name]:
                    ve.wait_ge(S("h_updated"), 1 + h_done[name])
                if name in norm_of:
                    norm_apply_vector(ve, norm_of[name], gain_of[name])
                if name == "s5in":
                    for q in range(QUARTERS):
                        split_lo(ve, n0 + 1, q, 1, 1)
                    sum_halves(ve, t0, 0, u[:, 0, :])
                    with ve.Fori(0, 3) as i:
                        for j in range(4):
                            s5_tile(i, j, True)
                    for j in range(4):
                        s5_tile(3, j, j < 3)
                    continue
                with ve.Fori(0, rounds - 1 if last_phase else rounds) as i:
                    for j in range(4):
                        splits(i, name, j)
                        if tiles == 4 or j % 2:
                            tile_post(name, i, j, j if tiles == 4 else j // 2)
                if last_phase:
                    for j in range(4):
                        if j < 3:
                            splits(rounds - 1, name, j)
                        if tiles == 4 or j % 2:
                            tile_post(name, rounds - 1, j, j if tiles == 4 else j // 2)
            ve.wait_ge(S("h_updated"), 1 + H_FINAL)
            norm_scale(ve, K_FINAL)
            for kt in range(KT):
                STT(h[:, kt, :], h[:, kt, :], vec[:, V_FIN + kt:V_FIN + kt + 1], rms[:, :], ALU.mult,
                    ALU.mult).then_inc(S("final_ready"), 1)


_INS = ["x", "p", "norm_mix", "norm_mlp", "norm_ple", "norm_final", "gdn_w_in", "gdn_conv_w", "gdn_a_log",
        "gdn_dt_bias", "gdn_o_norm", "gdn_w_out", "s5_w_in", "s5_lam_re", "s5_lam_im", "s5_log_step", "s5_b_re",
        "s5_b_im", "s5_c_re", "s5_c_im", "s5_d", "s5_w_out", "mlp_w_up", "mlp_w_down", "ple_w_proj", "ple_w_gate"]


def _constants():
    import numpy as np
    i = np.arange(P)
    row, col = i[:, None], i[None, :]
    same = row // 64 == col // 64
    below = row > col
    s32, s16 = row // 32 == col // 32, row // 16 == col // 16
    parts = [row == col, np.ones((P, P)), (row <= col) & same, same, -1.0 * (below & s16), below & s32 & ~s16,
             below & same & ~s32, np.broadcast_to(row < 64, (P, P)), np.broadcast_to(row >= 64, (P, P)),
             np.broadcast_to(np.arange(NT), (P, NT))]
    odd = (row // 16) % 2
    parts += [1 - odd, odd, odd - 1, -odd, np.full((P, 1), MAGIC), np.full((P, 1), 0.25), np.full((P, 1), EPS)]
    return np.ascontiguousarray(np.concatenate([np.asarray(a, np.float32) for a in parts], axis=1))


def kernel(**inputs):
    import numpy as _np
    import concourse.bacc as _bacc
    from concourse import mybir as _mybir
    from concourse.bass_utils import run_bass_kernel_spmd as _run

    nc = _bacc.Bacc("TRN2", target_bir_lowering=False, num_devices=1)
    arrays, tensors = {}, {}
    for name in _INS + ["constants"]:
        a = _constants() if name == "constants" else _np.ascontiguousarray(inputs[name])
        arrays[f"in_{name}_dram"] = a
        tensors[name] = nc.dram_tensor(f"in_{name}_dram", a.shape, _mybir.dt.from_np(a.dtype), kind="ExternalInput").ap()
    out = nc.dram_tensor("out_0_dram", (1, NT, D), _mybir.dt.float32, kind="ExternalOutput").ap()
    trunk(nc, tensors, out)
    r = _run(nc, [arrays], core_ids=[0])
    return r.results[0]["out_0_dram"]
```

```python
import math
from contextlib import ExitStack

import concourse.bass as bass
from concourse import mybir

ALU = mybir.AluOpType
ACT = mybir.ActivationFunctionType
F32 = mybir.dt.float32
F32R = mybir.dt.float32r
ds = bass.ds

P = 128
NT = 256
D = 2048
KT = D // P
FF = 4 * D
KH = 16
QUARTERS = 4
QK = KT // QUARTERS
EPS = 1e-6
MAGIC = 12582912.0

C_ID, C_ONE, C_U, C_SAME, C_M16, C_L1, C_L2, C_HALF, C_T, C_PAR = 0, 128, 256, 384, 512, 640, 768, 896, 1152, 1408
C_EPS = 1414

V_MIX, V_MLP, V_PLE, V_FIN, V_D = 0, 32, 64, 96, 112

H_BETA, H_GC, H_BEXP, H_KD, H_G, H_BHALF, H_GLAST, H_COLS = 0, 4, 8, 12, 16, 20, 24, 32

GDN_CHUNKS = 6 * KH
STAGES = 99
N_PARAMS = 20
TWO_PI_EXACT = 2 * math.pi
TWO_PI = 6.283185
PI_BELOW = 3.1415925
TP1, TP2 = 6.28125, 2029 / 2 ** 20
TP3 = 2 * math.pi - TP1 - TP2


class Sems:

    def __init__(self, nc, ctx):
        self._nc, self._ctx, self._made = nc, ctx, {}

    def __call__(self, name):
        if name not in self._made:
            self._made[name] = self._ctx.enter_context(self._nc.semaphore(name))
        return self._made[name]


def trunk(nc, t, out):
    with ExitStack() as ctx:
        S = Sems(nc, ctx)

        def sb(name, shape, dt=F32, scope=ctx):
            return scope.enter_context(nc.sbuf_tensor(name, shape, dt))

        bank = [ctx.enter_context(nc.psum_tensor(f"bank{i}", [P, 512], F32)) for i in range(8)]
        acc = bank[0:2]
        A, B, C, Dk, E, F = bank[2:8]

        act = sb("act", [P, KT, 2 * NT], F32R)
        g3 = ExitStack()
        sb("lower_half", [P, KT, 2 * NT], F32, g3)
        u = sb("u", [P, 2, NT], F32, g3)
        b_in = sb("b_in", [P, 2, 2, 4, 16], F32, g3)
        c_in = sb("c_in", [P, 2, 2, 64], F32, g3)
        b_t = sb("b_t", [P, 4, 64], F32, g3)
        b_blk = sb("b_blk", [P, 2, 4, 2, 16], F32, g3)
        c_blk = sb("c_blk", [P, 2, 2, 64], F32, g3)
        bT = sb("bT", [P, 2, P], F32, g3)
        cT = sb("cT", [P, 2, 2, P], F32, g3)
        turn = sb("turn", [P, 4, NT], F32, g3)
        rot = sb("rot", [P, 2, 4, NT], F32, g3)
        st, x1 = (sb(n, [P, 2, 2, NT], F32, g3) for n in ("st", "x1"))
        rb = sb("rb", [P, 2, NT], F32, g3)
        g3.close()
        g4 = ExitStack()
        sb("below_last_pair", [P, 2 * KT - 2, 2 * NT], F32, g4)
        tw = sb("tw", [P, 4, NT], F32, g4)
        g4.close()
        mid = sb("mid", [P, 2 * KT, 2 * NT], F32R)
        raw = [sb(f"raw{i}", [P, KT * P]) for i in range(3)]
        w_hi = [sb(f"w_hi{i}", [P, KT * P], F32R) for i in range(2)]
        w_lo = [sb(f"w_lo{i}", [P, KT * P], F32R) for i in range(2)]
        eps = sb("eps", [P, 1])
        tcol = sb("tcol", [P, 6])
        tq = sb("tq", [P, 2, 1])
        tiles_ = sb("tiles", [P, 6, NT])
        half = tiles_[:, 0:2, :]
        summed = tiles_[:, 2:4, :]
        tanh = tiles_[:, 4:6, :]
        cf = tiles_[:, 2:6, :].rearrange("p a n -> p (a n)").rearrange("p (c q) -> p c q", c=16)
        x2 = tiles_[:, 2:6, :].rearrange("p (s e) n -> p s e n", s=2)
        turning = tiles_[:, 2:4, :]
        consts = sb("consts", [P, 256])
        ident, ones = consts[:, 0:128], consts[:, 128:256]
        vec = sb("vec", [P, 128])
        s5v = sb("s5v", [P, 5, 64])
        onorm = sb("onorm", [P, 1])

        g1 = ExitStack()

        def gs(name, shape, dt=F32):
            return sb(name, shape, dt, g1)

        masks = gs("masks", [P, 5, P])
        U, SAME, M16N, ML1, ML2 = (masks[:, i, :] for i in range(5))
        conv_w = gs("conv_w", [P, 4, 64])
        gt = gs("gt", [P, KH, H_COLS])
        g0 = ExitStack()
        xn = sb("xn", [P, 2, D], F32, g0)
        h0 = sb("h0", [P, KT, NT], F32, g0)
        rows = sb("rows", [P, 5, P], F32, g0)
        ba_w = raw[2][:, 0:KT * 64]
        ga = sb("ga", [P, 12, 64], F32, g0)
        stat = sb("stat", [P, 16], F32, g0)
        ls2 = sb("ls2", [P, 2], F32, g0)
        abias = sb("abias", [P, 3, 32], F32, g0)
        halfsel = sb("halfsel", [P, 2 * P], F32, g0)
        g0.close()
        pre = gs("pre", [P, 4, NT + 4])
        y = gs("y", [P, 4, NT])
        z = gs("z", [P, 2, NT])
        conv_f = gs("conv_f", [P, 4, 4])
        hs = gs("hs", [P, H_COLS])
        T = [gs(f"T{i}", [P, 4, P]) for i in range(6)]
        L1, L2, RT, Vb, Kbe, kd, qeT = (gs(n, [P, 4, P]) for n in ("L1", "L2", "RT", "Vb", "Kbe", "kd", "qeT"))
        state = gs("state", [P, 2, P])
        g1.close()
        sq, Mp, P2, P8, WT, osq = (T[0],) * 6
        rn, Pm, P4, Dm, orn = (T[1],) * 5
        D1, PT, P4T, nW, oy = (T[2],) * 5
        erow, P2T, VN = (T[3],) * 3
        qkn = T[4]
        qkT = T[5]

        g2 = ExitStack()

        def ls(name, shape, dt=F32):
            return sb(name, shape, dt, g2)

        raw.append(ls("raw3", [P, KT * P]))
        h = ls("h", [P, KT, NT])
        sqb = ls("sqb", [P, 2, NT])
        rms = ls("rms", [P, NT])
        normed = ls("normed", [P, 2, NT])
        turn_abs, gl = sqb, normed
        pn = ls("pn", [P, 2, NT])
        pT = ls("pT", [P, 2, NT])
        wp = ls("wp", [P, 2, 2, P])
        row_out = ls("row_out", [P, 2, 512])
        g2.close()

        h_dram = nc.dram_tensor("h_scratch", (P, KT, NT), F32, kind="Internal").ap()
        turns_dram = nc.dram_tensor("turns_scratch", (KT, P, 4, NT), F32, kind="Internal").ap()
        w_in_d = t["gdn_w_in"][0].rearrange("(kt p) n -> p kt n", p=P)
        split4 = "(c kt p) n -> c p kt n"
        w_gout_d = t["gdn_w_out"][0].rearrange(split4, p=P, c=2)
        w_up_d = [t["mlp_w_up"][l].rearrange("(kt p) n -> p kt n", p=P) for l in range(2)]
        w_down_d = [t["mlp_w_down"][l].rearrange(split4, p=P, c=4) for l in range(2)]
        w_gate_d = [t["ple_w_gate"][l].rearrange("(kt p) n -> p kt n", p=P) for l in range(2)]
        w_pp_d = [t["ple_w_proj"][l].rearrange("(kt p) n -> p kt n", p=P) for l in range(2)]
        w_s5i_d = t["s5_w_in"][0].rearrange("(kt p) n -> p kt n", p=P)
        w_s5o_d = t["s5_w_out"][0].rearrange("(kt p) n -> p kt n", p=P)

        plan, n0, t0 = {}, GDN_CHUNKS, GDN_CHUNKS
        shapes = [("gout", 8, 4, 2)]
        for l in range(2):
            if l == 1:
                shapes += [("s5in", 4, 4, 4), ("s5out", 8, 4, 4)]
            for hf in range(2):
                shapes += [(f"up{l}{hf}", 8, 4, 4), (f"down{l}{hf}", 8, 4, 2)]
            shapes += [(f"ple{l}", 4, 4, 4)]
        if STAGES < 99:
            shapes = shapes[:STAGES]
        for name, rounds, chunks, tiles in shapes:
            plan[name] = (n0, t0, rounds, chunks, tiles)
            n0 += rounds * chunks
            t0 += rounds * tiles
        N_CHUNKS = n0

        def landed_before(n):
            if n < GDN_CHUNKS:
                return n // 3 + 1
            m = n - GDN_CHUNKS
            return m // 4 + 1 + (GDN_CHUNKS // 3 if m % 4 < 3 else 0)

        def raw_slot(n):
            return n % 3 if n < GDN_CHUNKS else (n - GDN_CHUNKS) % 4

        def load(sp, slot, src, split_done):
            if split_done is not None:
                sp.wait_ge(S("lo_ready"), split_done)
            sp.dma_start(raw[slot][:, :].rearrange("p (k n) -> p k n", k=KT), src).then_inc(S(f"raw_landed{slot}"), 16)

        def split_hi(eng, n, q, slot, landed, reused=True, par=None):
            if q == 0:
                eng.wait_ge(S(f"raw_landed{slot}"), 16 * landed)
            if reused:
                eng.wait_ge(S("weights_used"), 4 * n - 7 + q)
            c = slice(q * QK * P, (q + 1) * QK * P)
            eng.activation(w_hi[par][:, c], raw[slot][:, c], ACT.Copy).then_inc(S("hi_ready"), 1)

        def split_lo(eng, n, q, slot, par):
            eng.wait_ge(S("hi_ready"), 4 * n + q + 1)
            c = slice(q * QK * P, (q + 1) * QK * P)
            eng.tensor_tensor(w_lo[par][:, c], raw[slot][:, c], w_hi[par][:, c].bitcast(F32),
                              ALU.subtract).then_inc(S("lo_ready"), 1)

        def multiply(eng, n, q, par, tpar, rhs, k0=0, kend=KT, tile_free=None, last=False):
            if tile_free is not None:
                eng.wait_ge(S("acc_freed"), tile_free)
            eng.wait_ge(S("lo_ready"), 4 * n + q + 1)
            a = acc[tpar]
            for i in range(QK):
                kt = q * QK + i
                w = slice(kt * P, (kt + 1) * P)
                eng.matmul(a[:, :], w_hi[par][:, w], rhs[:, k0 + kt, :], start=(k0 + kt == 0), stop=False)
                mm = eng.matmul(a[:, 0:NT], w_lo[par][:, w], rhs[:, k0 + kt, 0:NT], start=False,
                                stop=(k0 + kt == kend - 1))
            mm.then_inc(S("weights_used"), 1)

        def half_copy(eng, n_end, tau, par, first=False):
            eng.wait_ge(S("weights_used"), 4 * n_end)
            if not first:
                eng.wait_ge(S("acc_freed"), tau - 1)
            eng.activation(half[:, par, :], acc[par][:, NT:2 * NT], ACT.Copy).then_inc(S("half_copied"), 1)

        def sum_halves(eng, tau, par, dst):
            eng.wait_ge(S("half_copied"), tau + 1)
            eng.tensor_tensor(dst, acc[par][:, 0:NT], half[:, par, :], ALU.add).then_inc(S("acc_freed"), 1)

        def norm_squares(eng, k, h_done):
            eng.wait_ge(S("h_updated"), 1 + h_done)
            with eng.Fori(0, KT // 2) as i:
                eng.wait_ge(S("sq_summed"), 1 + KT * k + 2 * i)
                for a in range(2):
                    eng.activation(sqb[:, a, :], h[:, ds(2 * i + a, 1), :], ACT.Square).then_inc(S("squared"), 1)
            eng.wait_ge(S("sq_summed"), 1 + KT * (k + 1))
            eng.activation(rms[:, :], F[:, 0:NT], ACT.Ln, scale=1.0 / D, bias=eps[:, 0:1]).then_inc(S("rms_log"), 1)
            eng.wait_ge(S("rms_log"), k + 1)
            eng.activation(rms[:, :], rms[:, :], ACT.Exp, scale=-0.5).then_inc(S("rms_ready"), 1)

        def norm_sums(eng, k):
            for kt in range(KT):
                eng.wait_ge(S("squared"), KT * k + kt + 1)
                eng.matmul(F[:, 0:NT], ones, sqb[:, kt % 2, :], start=(kt == 0),
                           stop=(kt == KT - 1)).then_inc(S("sq_summed"), 1)

        def norm_apply_vector(eng, k, gain):
            eng.wait_ge(S("rms_ready"), k + 1)
            with eng.Fori(0, KT // 2) as i:
                if k:
                    eng.wait_ge(S("act_ready"), 1 + KT * k + 2 * i)
                else:
                    eng.wait_ge(S("act_ready"), 1 + 2 * i)
                for a in range(2):
                    eng.scalar_tensor_tensor(normed[:, a, :], h[:, ds(2 * i + a, 1), :], vec[:, ds(2 * i + (gain + a), 1)],
                                             rms[:, :], ALU.mult, ALU.mult).then_inc(S("normed"), 1)
                for a in range(2):
                    eng.wait_ge(S("norm_hi"), KT * k + 2 * i + a + 1)
                    eng.tensor_tensor(act[:, ds(2 * i + a, 1), NT:2 * NT], normed[:, a, :],
                                      act[:, ds(2 * i + a, 1), 0:NT].bitcast(F32), ALU.subtract).then_inc(S("act_ready"), 1)

        def norm_apply_scalar(eng, k):
            with eng.Fori(0, KT // 2) as i:
                for a in range(2):
                    eng.wait_ge(S("normed"), KT * k + 2 * i + a + 1)
                    eng.activation(act[:, ds(2 * i + a, 1), 0:NT], normed[:, a, :], ACT.Copy).then_inc(S("norm_hi"), 1)

        def two_pairs_back(i, j, r4):
            pi = i * 16 + (4 * j + r4)
            return max(pi - 1, 0) + 1 if isinstance(pi, int) else pi

        def s5_rounds(eng, tile):
            for j in range(4):
                tile(0, j)
            with eng.Fori(1, 3) as i:
                for j in range(4):
                    tile(i, j)
            for j in range(4):
                tile(3, j)

        def ahead(i, j, d):
            return not isinstance(i, int) or 0 <= 4 * i + j + d < KT

        norm_of, h_done, upd = {}, {}, 0
        k = 0
        for name in plan:
            if name[:2] == "up" and name[3] == "0" or name[:3] == "ple" or name == "s5in":
                norm_of[name] = k
                k += 1
            h_done[name] = upd
            if name[:2] in ("go", "do", "pl") or name == "s5out":
                upd += 16
        K_FINAL, H_FINAL = k, upd
        gain_of = {"up00": V_MLP, "ple0": V_PLE, "s5in": V_MIX + 16, "up10": V_MLP + 16, "ple1": V_PLE + 16}

        block = ctx.enter_context(nc.Block())

        @block.sync
        def _(sp):
            sp.dma_start(xn[:, :, :], t["x"][0].rearrange("(b p) d -> p b d", p=P)).then_inc(S("x_in"), 16)
            par = [(consts[:, :], t["constants"][:, 0:256]),
                   (eps[:, :], t["constants"][:, C_EPS:C_EPS + 1]),
                   (masks[:, :, :], t["constants"][:, C_U:C_U + 640].rearrange("p (m q) -> p m q", m=5)),
                   (halfsel[:, :], t["constants"][:, C_HALF:C_HALF + 256]),
                   (rows[0:32, 0, :], t["norm_mix"].rearrange("l (k p) -> (l k) p", p=P)),
                   (rows[32:64, 0, :], t["norm_mlp"].rearrange("l (k p) -> (l k) p", p=P)),
                   (rows[64:96, 0, :], t["norm_ple"].rearrange("l (k p) -> (l k) p", p=P)),
                   (rows[96:112, 0, :], t["norm_final"].rearrange("(k p) -> k p", p=P)),
                   (rows[112:128, 0, :], t["s5_d"][0].rearrange("(k p) -> k p", p=P))]
            for tap in range(4):
                par.append((rows[64 * (tap % 2):64 * (tap % 2) + 64, 1 + tap // 2, :],
                            t["gdn_conv_w"][0][tap].rearrange("(k p) -> k p", p=P)))
            par += [(rows[0:64, 3, :], t["s5_lam_re"][0].rearrange("(q g) p -> q (g p)", g=2)),
                    (rows[64:128, 3, :], t["s5_lam_im"][0].rearrange("(q g) p -> q (g p)", g=2)),
                    (ls2[0:64, :], t["s5_log_step"][0].rearrange("(q g) -> q g", g=2)),
                    (abias[:, 0, :], t["gdn_a_log"].to_broadcast([P, 32])),
                    (abias[:, 1, :], t["gdn_dt_bias"].to_broadcast([P, 32])),
                    (onorm[:, :], t["gdn_o_norm"].rearrange("l (p o) -> (l p) o", o=1)),
                    (ba_w[:, :].rearrange("p (k n) -> p k n", k=KT), w_in_d[:, :, 12288:12352])]
            for dst, src in par:
                sp.dma_start(dst, src, allow_slow_non_contiguous=dst.shape[-1] == 1).then_inc(S("params_in"), 16)
            assert len(par) == N_PARAMS, len(par)
            for n, col in enumerate((0, 2048, 4096, 4096 + P)):
                if n == 2:
                    sp.wait_ge(S("ba_lo"), 1)
                load(sp, n % 3, w_in_d[:, :, col:col + P], 4 * (n - 2) if n >= 3 else None)
            sp.wait_ge(S("h0_ready"), 8)
            sp.dma_start(h_dram, h0[:, :, :]).then_inc(S("h_saved"), 16)
            with sp.Fori(0, KH - 1) as r:
                for c in range(6):
                    base = (8192, 8192 + P, P, 2048 + P, 4096 + 256, 4096 + 256 + P)[c]
                    step = 256 if c in (0, 1, 4, 5) else P
                    load(sp, (4 + c) % 3, w_in_d[:, :, ds(r * step + base, P)], 24 * r + 4 * (c + 2))
            for c in range(2):
                n = GDN_CHUNKS - 2 + c
                col = 8192 + 256 * (KH - 1) + P * c
                load(sp, n % 3, w_in_d[:, :, col:col + P], 4 * (n - 2))

            def gout_src(i, j):
                return w_gout_d[j % 2][:, :, ds(i * 256 + (j // 2) * P, P)] if not isinstance(i, int) else \
                    w_gout_d[j % 2][:, :, (2 * i + j // 2) * P:(2 * i + j // 2 + 1) * P]

            for j in range(4):
                n = GDN_CHUNKS + j
                if j == 3:
                    sp.wait_ge(S("mid_lo"), 1 + KH)
                    sp.wait_ge(S("h_saved"), 16)
                    sp.dma_start(h[:, :, :], h_dram).then_inc(S("h_loaded"), 16)
                    sp.dma_start(pn[:, :, :], t["p"][0][0].rearrange("(b p) e -> p b e", p=P)).then_inc(S("p_in"), 16)
                load(sp, j, gout_src(0, j), 4 * (n - 2))
            def b_and_c(ct, j, used):
                if used is not None:
                    sp.wait_ge(S("spread"), used)
                at = ds(ct, 1) if not isinstance(ct, int) else slice(ct, ct + 1)
                for ri, nm in enumerate(("re", "im")):
                    sp.dma_start(b_in[:, j % 2, ri, :, :], t[f"s5_b_{nm}"][0].rearrange(
                        "(c r g) p e -> c (g p) r e", g=2, r=4)[at][0]).then_inc(S(f"bc_in{j % 2}"), 16)
                    sp.dma_start(c_in[:, j % 2, ri, :], t[f"s5_c_{nm}"][0].rearrange(
                        "(c g) e p -> c (g e) p", g=8)[at][0]).then_inc(S(f"bc_in{j % 2}"), 16)

            def sub_loads(name, i, j):
                n0 = plan[name][0]
                col = lambda step, off: ds(i * step + off, P) if not isinstance(i, int) else slice(i * step + off, i * step + off + P)
                if name == "gout":
                    src = gout_src(i, j)
                elif name[:2] == "up":
                    src = w_up_d[int(name[2])][:, :, col(512, int(name[3]) * 4096 + j * P)]
                elif name[:4] == "down":
                    src = w_down_d[int(name[4])][2 * int(name[5]) + j % 2][:, :, col(256, (j // 2) * P)]
                elif name[:3] == "ple":
                    l = int(name[3])
                    src = w_gate_d[l][:, :, col(512, j * P)]
                    if l or not isinstance(i, int) or j >= 2:
                        sp.wait_ge(S("projected"), i * 4 + (16 * l + j - 1))
                    sp.dma_start(wp[:, j % 2, :, :], w_pp_d[l][:, :, col(512, j * P)]).then_inc(S(f"wp_in{j % 2}"), 16)
                elif name == "s5in":
                    src = w_s5i_d[:, :, col(512, j * P)]
                    if not isinstance(i, int):
                        b_and_c(i * 4 + (j - 2), j, i * 4 + (j - 3))
                else:
                    src = w_s5o_d[:, :, col(256, (j % 2) * D + (j // 2) * P)]
                load(sp, j, src, i * 16 + (4 * (n0 + j) - (12 if name != "gout" else 8)))

            for name, (n0, t0, rounds, chunks, tiles) in plan.items():
                first = 0
                if name in ("ple0", "s5in"):
                    first = 1
                    for j in range(4):
                        sub_loads(name, 0, j)
                    if name == "s5in":
                        sp.wait_ge(S("h_updated"), 1 + h_done["s5in"])
                        for j in range(2):
                            b_and_c(j, j, None)
                if name == "gout":
                    first = 1
                with sp.Fori(first, rounds) as i:
                    for j in range(4):
                        sub_loads(name, i, j)
                if name == "s5in":
                    for j in range(2):
                        b_and_c(KT - 2 + j, j, KT - 3 + j)
                if name == "ple0" and "ple1" in plan:
                    sp.wait_ge(S("p_turned"), 1)
                    sp.dma_start(pn[:, :, :], t["p"][1][0].rearrange("(b p) e -> p b e", p=P)).then_inc(S("p_in"), 16)
            for i in range(8):
                sp.wait_ge(S("row_ready"), i + 1)
                sp.dma_start(out[0].rearrange("(b p) d -> b p d", p=P)[i // 4][:, (i % 4) * 512:(i % 4 + 1) * 512],
                             row_out[:, i % 2, :]).then_inc(S(f"stored{i % 2}"), 16)
            for a in range(2):
                sp.wait_ge(S(f"stored{a}"), 64)

        @block.tensor
        def _(pe):
            for name in ("sq_summed", "bc_turned", "y_done", "x1_used"):
                pe.sem_inc(S(name), 1)
            pe.wait_ge(S("params_in"), 16 * N_PARAMS)
            for i in range(4):
                mm = pe.transpose(A[:, i * P:(i + 1) * P], rows[:, i, :], ident)
            mm.then_inc(S("vectors_turned"), 1)
            pe.wait_ge(S("steps_ready"), 1)
            pe.transpose(B[:, 0:64], rows[0:64, 4, :], ident[0:64, 0:64]).then_inc(S("vectors_turned"), 1)
            for again in range(2):
                if again:
                    pe.wait_ge(S("x_scaled"), 2)
                else:
                    pe.wait_ge(S("x_in"), 16)
                for g in range(8):
                    bk = (C, Dk, E, F)[g % 4]
                    if again:
                        pe.wait_ge(S("act_ready0"), 2 * (g - 4) + 2 if g >= 4 else 0)
                        pe.wait_ge(S("h0_ready"), 8)
                    elif g >= 4:
                        pe.wait_ge(S("h0_ready"), g - 3)
                    for a in range(2):
                        for b in range(2):
                            mm = pe.transpose(bk[:, a * NT + b * P:a * NT + (b + 1) * P],
                                              xn[:, b, (2 * g + a) * P:(2 * g + a + 1) * P], ident)
                    mm.then_inc(S("x_turned"), 1)
            pe.wait_ge(S("act_ready0"), KT)
            pe.wait_ge(S("ba_lo"), 1)
            pe.wait_ge(S("vectors_ready"), 2)
            bh = mid[:, 0:2, :].rearrange("p a n -> p (a n)").rearrange("p (k n) -> p k n", k=KT)
            bl = mid[:, 2:4, :].rearrange("p a n -> p (a n)").rearrange("p (k n) -> p k n", k=KT)
            for b in range(2):
                for kt in range(KT):
                    x_hi, x_lo = act[:, kt, b * P:(b + 1) * P], act[:, kt, NT + b * P:NT + (b + 1) * P]
                    pe.matmul(A[:, b * 64:(b + 1) * 64], x_hi, bh[:, kt, :], start=(kt == 0), stop=False)
                    pe.matmul(A[:, b * 64:(b + 1) * 64], x_lo, bh[:, kt, :], start=False, stop=False)
                    mm = pe.matmul(A[:, b * 64:(b + 1) * 64], x_hi, bl[:, kt, :], start=False, stop=(kt == KT - 1))
            mm.then_inc(S("ba_done"), 1)
            for n in range(4):
                for q in range(QUARTERS):
                    multiply(pe, n, q, n % 2, n % 2, act, tile_free=(n - 1) if (n >= 2 and q == 0) else None)
                if n == 0:
                    pe.wait_ge(S("setup_vectors"), 7)
                    g_all = ga[:, 8, :]
                    pe.matmul(B[:, 0:64], U, g_all, start=True, stop=True)
                    pe.matmul(B[:, 64:128], SAME, g_all, start=True, stop=True)
                    for hc in range(2):
                        mm = pe.matmul(B[:, 128 + 64 * hc:192 + 64 * hc], halfsel[:, hc * P:(hc + 1) * P], g_all,
                                       start=True, stop=True)
                    mm.then_inc(S("gc_done"), 1)

            def four(bk, lhs, rhs, name, turn_=False):
                for m in range(4):
                    if turn_:
                        mm = pe.transpose(bk[:, m * P:(m + 1) * P], lhs[:, m, :], ident)
                    else:
                        mm = pe.matmul(bk[:, m * P:(m + 1) * P], lhs[:, m, :], rhs[:, m, :], start=True, stop=True)
                mm.then_inc(S(name), 1)

            def out_chunk(r, c):
                b, lo = c // 2, 64 * (c % 2)
                for hd in range(2):
                    dst = B[:, hd * NT + 64 * c:hd * NT + 64 * (c + 1)]
                    if c:
                        pe.matmul(dst, state[:, hd, :], qeT[:, 2 * b + hd, lo:lo + 64], start=True, stop=False)
                    mm = pe.matmul(dst, VN[lo:lo + 64, 2 * b + hd, :], qkT[lo:lo + 64, 2 * b + hd, lo:lo + 64],
                                   start=(c == 0), stop=True)
                return mm

            def state_add(c):
                b, lo = c // 2, 64 * (c % 2)
                for hd in range(2):
                    mm = pe.matmul(C[:, hd * P:(hd + 1) * P], kd[lo:lo + 64, 2 * b + hd, :],
                                   VN[lo:lo + 64, 2 * b + hd, :], start=True, stop=True)
                mm.then_inc(S("kv_done"), 1)

            def state_read(r, c):
                b, lo = c // 2, 64 * (c % 2)
                pe.wait_ge(S("state_ready"), 3 * r + c)
                for hd in range(2):
                    mm = pe.matmul(A[lo:lo + 64, hd * P:(hd + 1) * P], nW[:, 2 * b + hd, lo:lo + 64],
                                   state[:, hd, :], start=True, stop=True)
                mm.then_inc(S("ws_done"), 1)

            kq = qkn[:, :, :].rearrange("p (a b) q -> p a b q", a=2)

            def squared_lengths(r):
                pe.wait_ge(S("sq_ready"), r + 1)
                pe.matmul(Dk[:, :], ones, sq[:, :, :].rearrange("p m q -> p (m q)"), start=True, stop=True).then_inc(S("ssum"), 1)

            def core(r, s):
                w = lambda name, k=1, o=1: pe.wait_ge(S(name), k * r + o)
                if s == 0:
                    w("hs_ready")
                    for m in range(4):
                        mm = pe.matmul(C[:, m * P:(m + 1) * P], hs[:, H_G + m:H_G + m + 1].to_broadcast([P, P]), U,
                                       start=True, stop=True)
                    mm.then_inc(S("gcrow"), 1)
                elif s == 1:
                    w("qkn_ready")
                    w("o_normed")
                    for b in range(2):
                        mm = pe.matmul(B[:, b * NT:(b + 1) * NT], kq[:, 1, b, :], kq[:, :, b, :], start=True, stop=True)
                    mm.then_inc(S("attn_done"), 1)
                elif s == 2:
                    pe.wait_ge(S("gated"), 6 * r + 4)
                    w("lengths_read")
                    for b in range(2):
                        for hd in range(2):
                            pe.transpose(Dk[:, (2 * b + hd) * P:(2 * b + hd + 1) * P], y[:, 2 + hd, b * P:(b + 1) * P], ident)
                        mm = pe.transpose(E[:, b * P:(b + 1) * P], kq[:, 1, b, :], ident)
                    mm.then_inc(S("vk_turned"), 1)
                elif s == 3:
                    w("P_ready")
                    four(A, Pm, None, "PT_turned", True)
                elif s == 4:
                    w("PT_ready")
                    four(C, PT, Pm, "P2_done")
                    four(F, Pm, PT, "P2T_done")
                elif s == 5:
                    w("P2_ready")
                    w("RT_ready", 6, 1)
                    four(A, P2, RT, "R_done")
                    w("P2T_ready")
                    four(C, P2T, P2, "P4_done")
                    four(F, P2, P2T, "P4T_done")
                elif s == 6:
                    w("P4_ready")
                    w("RT_ready", 6, 2)
                    four(A, P4, RT, "R_done")
                    w("P4T_ready")
                    four(C, P4T, P4, "P8_done")
                elif s == 7:
                    w("P8_ready")
                    w("RT_ready", 6, 3)
                    four(A, P8, RT, "R_done")
                elif s == 8:
                    w("RT_ready", 6, 4)
                    four(C, RT, None, "D1_turned", True)
                elif s == 9:
                    w("L_ready")
                    four(A, L1, RT, "W1_done")
                elif s == 10:
                    w("Dm_ready", 2)
                    w("WT_ready", 2)
                    four(C, Dm, WT, "R_done")
                elif s == 11:
                    w("RT_ready", 6, 5)
                    four(A, RT, None, "D2_turned", True)
                    four(F, L2, RT, "W2_done")
                elif s == 12:
                    w("Dm_ready", 2, 2)
                    w("WT_ready", 2, 2)
                    four(C, Dm, WT, "R_done")
                elif s == 13:
                    w("RT_ready", 6, 6)
                    w("Vb_ready")
                    four(A, RT, Vb, "U_done")
                    w("Kbe_ready")
                    four(F, Kbe, RT, "W_done")
                elif s == 14:
                    w("VN_ready")
                    w("qkT_ready")
                    out_chunk(r, 0)
                    w("kd_ready")
                    state_add(0)
                elif s in (15, 17, 19):
                    if s == 15:
                        w("nW_ready")
                    state_read(r, (s - 13) // 2)
                elif s in (16, 18, 20):
                    c = (s - 14) // 2
                    if c == 1:
                        w("qeT_ready")
                    pe.wait_ge(S("vn_ready"), 3 * r + c)
                    mm = out_chunk(r, c)
                    if c < 3:
                        state_add(c)
                    else:
                        mm.then_inc(S("ot_done"), 1)
                elif s == 21:
                    w("osq_ready")
                    pe.matmul(E[:, :], ones, osq[:, :, :].rearrange("p m q -> p (m q)"), start=True, stop=True).then_inc(S("osum_done"), 1)

            def head(r, last):
                for s in range(24):
                    if s < 8 or not last:
                        c, q = s // 4, s % 4
                        n = 6 * r + 4 + c
                        multiply(pe, n, q, c % 2, c % 2, act, tile_free=n - 1 if q == 0 else None)
                    core(r, s)
                    if s == 18 and not last:
                        squared_lengths(r + 1)

            squared_lengths(0)
            with pe.Fori(0, KH - 1) as r:
                head(r, False)
            head(KH - 1, True)

            def turn_p(l):
                pe.wait_ge(S("p_in"), 16 * (l + 1))
                for e in range(2):
                    for b in range(2):
                        mm = pe.transpose(E[:, e * NT + b * P:e * NT + (b + 1) * P], pn[:, b, e * P:(e + 1) * P], ident)
                mm.then_inc(S("p_turned"), 1)

            def turn_blocks(ct):
                pe.wait_ge(S("spread"), ct + 1)
                if not isinstance(ct, int) or ct:
                    pe.wait_ge(S("bcT_ready"), ct)
                for a in range(2):
                    pe.transpose(B[:, a * P:(a + 1) * P], b_blk[:, a, :, :, :].rearrange("p r g e -> p (r g e)"), ident)
                for a in range(2):
                    mm = pe.transpose(B[:, (2 + a) * P:(3 + a) * P], c_blk[:, a, :, :].rearrange("p g e -> p (g e)"), ident)
                mm.then_inc(S("bc_turned"), 1)

            def state_inputs(ct, j, r4s):
                if r4s[0] == 0:
                    pe.wait_ge(S("bcT_ready"), ct + 1)
                    pe.wait_ge(S("acc_freed"), plan["s5in"][1] + ct + 1)
                for r4 in r4s:
                    if not isinstance(ct, int) or ct:
                        pe.wait_ge(S("bu_products"), ct * 4 + (r4 - 3))
                    bk = (C, Dk, E, F)[r4]
                    for a in range(2):
                        mm = pe.matmul(bk[:, a * NT:(a + 1) * NT], bT[32 * r4:32 * r4 + 32, a, :],
                                       u[32 * r4:32 * r4 + 32, j % 2, :], start=True, stop=True)
                    mm.then_inc(S("bu_done"), 1)

            def s5_in_tile(i, j):
                n0, t0 = plan["s5in"][0:2]
                ct = i * 4 + j
                for r4 in range(4):
                    for q in ((0, 1), (2,), (3,), ())[r4]:
                        if ahead(i, j, 2):
                            multiply(pe, ct + (n0 + 2), q, j % 2, j % 2, act,
                                     tile_free=ct + (t0 + 1) if q == 0 else None)
                        if q == 0 and ahead(i, j, 1):
                            turn_blocks(ct + 1)
                    if r4 >= 2 and ahead(i, j, 1):
                        state_inputs(ct + 1, j + 1, (2 * r4 - 4, 2 * r4 - 3))
                    pe.wait_ge(S("x1_ready"), ct * 4 + (r4 + 2))
                    if r4 == 0:
                        pe.wait_ge(S("gelu_in"), ct + 1)
                    dst = A[32 * r4:32 * r4 + 32, 0:NT]
                    cre, cim = (cT[:, j % 2, e, 32 * r4:32 * r4 + 32] for e in range(2))
                    pe.matmul(dst, cre, x1[:, r4 % 2, 0, :], start=True, stop=False)
                    pe.matmul(dst, cim, x1[:, r4 % 2, 1, :], start=False, stop=False).then_inc(S("x1_used"), 1)
                    pe.wait_ge(S("x2_ready"), ct * 4 + (r4 + 2))
                    pe.matmul(dst, cre, x2[:, r4 % 2, 1, :], start=False, stop=False)
                    pe.matmul(dst, cim, x2[:, r4 % 2, 0, :], start=False, stop=True).then_inc(S("y_done"), 1)

            for name, (n0, t0, rounds, chunks, tiles) in plan.items():
                if name in norm_of:
                    k = norm_of[name]
                    norm_sums(pe, k)
                if name[:3] == "ple":
                    turn_p(int(name[3]))
                    pe.wait_ge(S("pT_ready"), int(name[3]) + 1)
                if name == "s5in":
                    turn_blocks(0)
                    for q in range(QUARTERS):
                        pe.wait_ge(S("act_ready"), 1 + KT * norm_of[name] + QK * (q + 1))
                        multiply(pe, n0, q, 0, 0, act, tile_free=t0 - 1 if q == 0 else None)
                    for q in range(QUARTERS):
                        multiply(pe, n0 + 1, q, 1, 1, act, tile_free=t0 if q == 0 else None)
                    state_inputs(0, 0, (0, 1, 2, 3))
                    s5_rounds(pe, s5_in_tile)
                    continue
                with pe.Fori(0, rounds) as i:
                    for j in range(4):
                        n = i * 4 + (n0 + j)
                        two = tiles == 2
                        tj = j // 2 if two else j
                        tau = i * tiles + (t0 + tj)
                        for q in range(QUARTERS):
                            if name in norm_of and j == 0:
                                pe.wait_ge(S("act_ready"), 1 + KT * norm_of[name] + QK * (q + 1))
                            if name == "gout" and j == 0 and q == 0:
                                pe.wait_ge(S("mid_lo"), 1 + KH)
                            if name[:4] == "down" and j == 0 and q == 0:
                                pe.wait_ge(S("hidden_lo"), 1 + 32 * (2 * int(name[4]) + int(name[5]) + 1))
                            if name == "s5out" and j == 0 and q == 0:
                                pe.wait_ge(S("s5_lo"), 1 + KT)
                            multiply(pe, n, q, j % 2, tj % 2, act if tiles == 4 and name != "s5out" else mid,
                                     k0=KT * (j % 2) if two else 0, kend=2 * KT if two else KT,
                                     tile_free=tau - 1 if q == 0 and (not two or j % 2 == 0) else None)
                        if name[:3] == "ple":
                            l = int(name[3])
                            ct = 4 * i + j
                            pe.wait_ge(S(f"wp_in{j % 2}"), 16 * (8 * l + 1 + j // 2) + 32 * i)
                            if l or j >= 2:
                                pe.wait_ge(S("proj_read"), 1 + 16 * l + 4 * i + j - 1)
                            else:
                                pe.wait_ge(S("proj_read"), 1 + 4 * i)
                            pe.matmul((C, Dk)[j % 2][:, 0:NT], wp[:, j % 2, 0, :], pT[:, 0, :], start=True, stop=False)
                            pe.matmul((C, Dk)[j % 2][:, 0:NT], wp[:, j % 2, 1, :], pT[:, 1, :], start=False,
                                      stop=True).then_inc(S("projected"), 1)
            norm_sums(pe, K_FINAL)
            for g in range(8):
                b, c4 = g // 4, g % 4
                pe.wait_ge(S("final_ready"), KT)
                if g >= 2:
                    pe.wait_ge(S("row_ready"), g - 1)
                for a in range(4):
                    mm = pe.transpose((A, B)[g % 2][:, a * P:(a + 1) * P], h[:, 4 * c4 + a, b * P:(b + 1) * P], ident)
                mm.then_inc(S("row_turned"), 1)

        @block.scalar
        def _(se):
            for name in ("rot_ready",):
                se.sem_inc(S(name), 1)
            link_n = [0]

            def link(ins):
                link_n[0] += 1
                ins.then_inc(S("scalar_setup"), 1)
                se.wait_ge(S("scalar_setup"), link_n[0])
                return ins

            def A_(dst, src, f=ACT.Copy, **kw):
                return se.activation(dst, src, f, **kw)

            for q in range(QUARTERS):
                split_hi(se, 0, q, 0, 1, reused=False, par=0)
            se.wait_ge(S("x_in"), 16)
            for b in range(2):
                mm = A_(h0[:, 8 * b:8 * b + 8, :].rearrange("p k n -> p (k n)"), xn[:, b, :], ACT.Square,
                        accum_out=stat[:, b:b + 1])
                mm.then_inc(S("x_squared"), 1)
            se.wait_ge(S("x_squared"), 2)
            se.wait_ge(S("params_in"), 16 * N_PARAMS)
            A_(stat[:, 2:4], stat[:, 0:2], ACT.Sqrt, scale=1.0 / D, bias=eps[:, 0:1]).then_inc(S("x_squared"), 1)
            se.wait_ge(S("vectors_turned"), 2)
            A_(vec[:, :], A[:, 0:P])
            A_(conv_w[:, :, :].rearrange("p a b -> p (a b)"), A[:, P:3 * P])
            link(A_(cf[:, 0:2, :].rearrange("p a b -> p (a b)"), A[:, 3 * P:4 * P]))
            A_(cf[:, 2, :], B[:, 0:64], ACT.Exp).then_inc(S("vectors_ready"), 2)
            for g in range(8):
                se.wait_ge(S("x_turned"), g + 1)
                se.wait_ge(S("x_squared"), 2)
                A_(h0[:, 2 * g:2 * g + 2, :].rearrange("p k n -> p (k n)"), (C, Dk, E, F)[g % 4][:, :]).then_inc(S("h0_ready"), 1)
            bh = mid[:, 0:2, :].rearrange("p a n -> p (a n)")
            A_(bh, ba_w[:, :]).then_inc(S("ba_hi"), 1)
            se.wait_ge(S("vectors_ready"), 2)
            for kt in range(KT):
                se.wait_ge(S("x_turned"), 8 + kt // 2 + 1)
                A_(act[:, kt, 0:NT], (C, Dk, E, F)[kt // 2 % 4][:, (kt % 2) * NT:(kt % 2 + 1) * NT],
                   scale=vec[:, V_MIX + kt:V_MIX + kt + 1]).then_inc(S("x_hi"), 1)
            se.wait_ge(S("setup_vectors"), 1)
            A_(cf[:, 5, :], cf[:, 4, :], ACT.Exp).then_inc(S("setup_functions"), 1)
            se.wait_ge(S("setup_vectors"), 2)
            A_(cf[:, 11, :], cf[:, 10, :], ACT.Sin)
            A_(cf[:, 12, :], cf[:, 10, :], ACT.Sin, scale=0.5).then_inc(S("setup_functions"), 1)
            se.wait_ge(S("setup_vectors"), 3)
            A_(cf[:, 13, :], cf[:, 13, :], ACT.Sin).then_inc(S("setup_functions"), 1)
            se.wait_ge(S("ba_done"), 1)
            v = A[:, 0:P].rearrange("p (b k h) -> p b k h", b=2, k=2)
            gv = lambda i: ga[:, i, :].rearrange("p (b h) -> p b h", b=2)
            A_(gv(0), v[:, :, 0, :], ACT.Exp, scale=-1.0).then_inc(S("setup_functions"), 1)
            A_(abias[:, 2, :], abias[:, 0, :], ACT.Exp).then_inc(S("setup_functions"), 1)
            se.wait_ge(S("setup_vectors"), 5)
            A_(ga[:, 5, :], ga[:, 4, :], ACT.Exp, scale=-1.0).then_inc(S("setup_functions"), 1)
            se.wait_ge(S("setup_vectors"), 6)
            A_(ga[:, 6, :], ga[:, 5, :], ACT.Ln).then_inc(S("setup_functions"), 1)
            se.wait_ge(S("gc_done"), 1)
            A_(ga[:, 9, :], B[:, 0:64], ACT.Exp)
            A_(ga[:, 1, :], B[:, 128:192], ACT.Exp)
            A_(ga[:, 3, :], B[:, 192:256], ACT.Exp).then_inc(S("setup_functions"), 1)
            se.wait_ge(S("setup_vectors"), 8)
            A_(ga[:, 11, :], ga[:, 11, :], ACT.Exp).then_inc(S("setup_functions"), 1)

            def gate_tanh(n, par, src, ready, v_ready, first=False):
                se.wait_ge(S(ready), v_ready)
                if not first:
                    se.wait_ge(S("gated"), n - 1)
                A_(tanh[:, par, :], src, ACT.Tanh, scale=0.5).then_inc(S("tanh_ready"), 1)

            def front(hd, j, first=False):
                n = 6 * hd + j
                half_copy(se, n + 1, n, j % 2, first=first)
                gate_tanh(n, j % 2, y[:, j, :], "conv_done", 4 * hd + j + 1, first)

            def front_z(r, j):
                n = 6 * r + 4 + j
                half_copy(se, n + 1, n, j)
                gate_tanh(n, j, z[:, j, :], "acc_freed", n + 1)

            for n in range(4):
                for q in range(QUARTERS):
                    split_hi(se, n + 1, q, (n + 1) % 3, (n + 1) // 3 + 1, reused=n + 1 >= 2, par=(n + 1) % 2)
                if n < 3:
                    front(0, n, first=n < 2)

            def squares(r):
                se.wait_ge(S("gated"), 6 * r + 2)
                A_(sq[:, :, :].rearrange("p m q -> p (m q)"), y[:, 0:2, :].rearrange("p a n -> p (a n)"),
                   ACT.Square).then_inc(S("sq_ready"), 1)

            def inverse_lengths(r):
                se.wait_ge(S("ssum"), r + 1)
                rn_ = rn[:, :, :].rearrange("p m q -> p (m q)")
                A_(rn_, Dk[:, :], ACT.Ln, scale=0.25, bias=eps[:, 0:1]).then_inc(S("lengths_read"), 1)
                se.wait_ge(S("lengths_read"), r + 1)
                A_(rn_, rn_, ACT.Exp, scale=-0.5).then_inc(S("qk_inverse"), 1)

            def core(r, s):
                w = lambda name, k=1, o=1: se.wait_ge(S(name), k * r + o)
                fl = lambda a: a[:, :, :].rearrange("p m q -> p (m q)")
                if s == 0:
                    w("gcrow")
                    A_(fl(erow), C[:, :], ACT.Exp).then_inc(S("erow_ready"), 1)
                elif s == 1:
                    w("d1_ready")
                    A_(fl(D1), fl(D1), ACT.Exp, scale=-1.0).then_inc(S("D1_ready"), 1)
                    w("d2_ready")
                    A_(fl(qkT), fl(qkT), ACT.Exp).then_inc(S("D2_ready"), 1)
                elif s == 3:
                    w("PT_turned")
                    A_(fl(PT), A[:, :]).then_inc(S("PT_ready"), 1)
                    w("hs_ready")
                    w("vk_turned")
                    for m in range(4):
                        mm = A_(Vb[:, m, :], Dk[:, m * P:(m + 1) * P], scale=hs[:, H_BHALF + m:H_BHALF + m + 1])
                    mm.then_inc(S("Vb_ready"), 1)
                elif s == 4:
                    w("P2_done")
                    w("L_ready")
                    A_(fl(P2), C[:, :]).then_inc(S("P2_ready"), 1)
                    for m in range(4):
                        mm = A_(Kbe[:, m, :], E[:, (m // 2) * P:(m // 2 + 1) * P], scale=hs[:, H_BEXP + m:H_BEXP + m + 1])
                    mm.then_inc(S("Kbe_ready"), 1)
                elif s == 5:
                    w("P4_done")
                    A_(fl(P4), C[:, :]).then_inc(S("P4_ready"), 1)
                    for m in range(4):
                        mm = A_(kd[:, m, :], E[:, (m // 2) * P:(m // 2 + 1) * P], scale=hs[:, H_KD + m:H_KD + m + 1])
                    mm.then_inc(S("kd_ready"), 1)
                elif s == 6:
                    w("P8_done")
                    A_(fl(P8), C[:, :]).then_inc(S("P8_ready"), 1)
                elif s == 8:
                    w("D1_turned")
                    A_(fl(Dm), C[:, :]).then_inc(S("Dm_ready"), 1)
                elif s == 9:
                    w("W1_done")
                    A_(fl(WT), A[:, :]).then_inc(S("WT_ready"), 1)
                elif s == 11:
                    w("D2_turned")
                    A_(fl(Dm), A[:, :]).then_inc(S("Dm_ready"), 1)
                    w("W2_done")
                    A_(fl(WT), F[:, :]).then_inc(S("WT_ready"), 1)
                elif s == 13:
                    w("W_done")
                    A_(fl(nW), F[:, :], scale=-1.0).then_inc(S("nW_ready"), 1)
                elif s == 20:
                    w("ot_done")
                    A_(fl(osq), B[:, :], ACT.Square).then_inc(S("osq_ready"), 1)
                elif s == 21:
                    w("osum_done")
                    if not (isinstance(r, int) and r == KH - 1):
                        w("qkn_ready", 1, 2)
                    A_(fl(orn), E[:, :], ACT.Ln, scale=1.0 / (128 * 128), bias=eps[:, 0:1]).then_inc(S("o_log"), 1)
                    w("o_log")
                    A_(fl(orn), fl(orn), ACT.Exp, scale=-0.5).then_inc(S("o_inverse"), 1)
                elif s == 22:
                    w("oy_ready")
                    A_(mid[:, ds(2 * r, 2), 0:NT] if not isinstance(r, int) else mid[:, 2 * r:2 * r + 2, 0:NT],
                       oy[:, :, :].rearrange("p (a m) q -> p a (m q)", a=2)).then_inc(S("mid_hi"), 1)

            def head(r, last):
                for s in range(24):
                    if s < 8 or not last:
                        c, q = s // 4, s % 4
                        m = 5 + c
                        if last and c == 1:
                            split_hi(se, GDN_CHUNKS, q, 0, landed_before(GDN_CHUNKS), par=0)
                        else:
                            split_hi(se, 6 * r + m, q, m % 3, 2 * r + m // 3 + 1, par=m % 2)
                    if s in (4, 8):
                        front_z(r, s // 4 - 1)
                    if s in (12, 16, 20) and not last:
                        front(r + 1, s // 4 - 3)
                    core(r, s)
                    if s == 0:
                        front(r, 3)
                    if s == 17 and not last:
                        squares(r + 1)
                    if s == 19 and not last:
                        inverse_lengths(r + 1)

            squares(0)
            inverse_lengths(0)
            with se.Fori(0, KH - 1) as r:
                head(r, False)
            for a in range(2):
                se.wait_ge(S(f"turn_saved{a}"), 16 * 2 * KT)
            head(KH - 1, True)

            def next_hi(i, name, j, nxt_first):
                n0 = plan[name][0]
                s = (j + 1) % 4
                landed = i + (landed_before(n0 + j + 1))
                return n0 + j + 1, s, landed

            def splits(i, name, j):
                n0, t0, rounds, chunks, tiles = plan[name]
                s = (j + 1) % 4
                n = i * 4 + (n0 + j + 1)
                for q in range(QUARTERS):
                    split_hi(se, n, q, s, i + landed_before(n0 + j + 1), par=(j + 1) % 2)

            def tile_post(name, i, j, tj):
                n0, t0, rounds, chunks, tiles = plan[name]
                tau = i * tiles + (t0 + tj)
                half_copy(se, i * 4 + (n0 + j + 1), tau, tj % 2)
                if name[:2] == "up":
                    tile = 32 * (2 * int(name[2]) + int(name[3]))
                    se.wait_ge(S("hidden"), i * 4 + (tile + j + 1))
                    A_(mid[:, ds(i * 4 + j, 1), 0:NT], normed[:, j % 2, :]).then_inc(S("hidden_hi"), 1)
                elif name[:3] == "ple":
                    se.wait_ge(S("acc_freed"), tau + 1)
                    A_(tanh[:, j % 2, :], summed[:, j % 2, :], ACT.Tanh, scale=0.5).then_inc(S("gate_tanh"), 1)
                elif name == "s5out" and j % 2:
                    se.wait_ge(S("acc_freed"), tau + 1)
                    A_(tanh[:, 1, :], summed[:, 1, :], ACT.Tanh, scale=0.5).then_inc(S("glu_tanh"), 1)

            def blocks_turned(ct, j):
                se.wait_ge(S("bc_turned"), ct + 2)
                if not isinstance(ct, int) or ct:
                    se.wait_ge(S("bu_done"), ct * 4)
                if not isinstance(ct, int) or ct >= 2:
                    se.wait_ge(S("y_done"), ct * 4 - 3)
                A_(bT[:, :, :].rearrange("p a q -> p (a q)"), B[:, 0:NT])
                A_(cT[:, j % 2, :, :].rearrange("p a q -> p (a q)"), B[:, NT:2 * NT]).then_inc(S("bcT_ready"), 1)

            def gelu(step, ct):
                if step == 0:
                    se.wait_ge(S("gelu_in"), ct + 2)
                    A_(gl[:, 1, :], gl[:, 0, :], ACT.Square).then_inc(S("gelu_sq"), 1)
                elif step == 1:
                    se.wait_ge(S("gelu_arg"), ct + 1)
                    A_(gl[:, 1, :], gl[:, 1, :], ACT.Tanh, scale=math.sqrt(2 / math.pi)).then_inc(S("gelu_tanh"), 1)
                else:
                    se.wait_ge(S("gelu_ready"), ct + 1)
                    A_(mid[:, ds(ct, 1), 0:NT] if not isinstance(ct, int) else mid[:, ct:ct + 1, 0:NT], gl[:, 0, :],
                       scale=0.5).then_inc(S("s5_hi"), 1)

            def s5_tile(i, j):
                n0, t0 = plan["s5in"][0:2]
                ct = i * 4 + j
                for r4 in range(4):
                    a = r4 % 2
                    if not a:
                        se.wait_ge(S(f"turn_in{r4 // 2}"), ct * 16 + 16)
                    before = two_pairs_back(i, j, r4)
                    se.wait_ge(S("rot_ready"), before)
                    A_(turn_abs[:, a, :], turn[:, r4, :], ACT.Abs).then_inc(S("turn_size"), 1)
                    se.wait_ge(S("x1_ready"), before)
                    se.wait_ge(S("x2_ready"), before)
                    for e, sign in ((1, -1), (2, 1), (3, -1)):
                        A_(rot[:, a, e, :], turn[:, r4, :], ACT.Sin, scale=sign * TWO_PI)
                    se.wait_ge(S("turn_size"), ct * 4 + (r4 + 1))
                    A_(rot[:, a, 0, :], turn_abs[:, a, :], ACT.Sin, scale=-TWO_PI,
                       bias=tcol[:, 5:6]).then_inc(S("rot_ready"), 1)
                    if ahead(i, j, 2):
                        split_hi(se, ct + (n0 + 3), r4, (j + 3) % 4, i + landed_before(n0 + j + 3), par=(j + 1) % 2)
                    if r4 == 0 and ahead(i, j, 1):
                        half_copy(se, ct + (n0 + 2), ct + (t0 + 1), (j + 1) % 2)
                    if r4 == 1 and ahead(i, j, 1):
                        blocks_turned(ct + 1, j + 1)
                    if r4 == 0 and ahead(i, j, -2):
                        gelu(2, ct - 2)
                    if r4 >= 2 and ahead(i, j, -1):
                        gelu(r4 - 2, ct - 1)

            for name, (n0, t0, rounds, chunks, tiles) in plan.items():
                last_phase = name == list(plan)[-1]
                if name in norm_of:
                    k = norm_of[name]
                    norm_squares(se, k, h_done[name])
                    norm_apply_scalar(se, k)
                if name[:3] == "ple":
                    l = int(name[3])
                    se.wait_ge(S("p_turned"), l + 1)
                    A_(pT[:, :, :].rearrange("p e n -> p (e n)"), E[:, :]).then_inc(S("pT_ready"), 1)
                if name == "s5in":
                    for c in (1, 2):
                        for q in range(QUARTERS):
                            split_hi(se, n0 + c, q, c, landed_before(n0 + c), par=c % 2)
                        if c == 1:
                            half_copy(se, n0 + 1, t0, 0)
                            se.wait_ge(S("t_in"), 16)
                            blocks_turned(0, 0)
                    s5_rounds(se, s5_tile)
                    gelu(2, KT - 2)
                    for step in range(3):
                        gelu(step, KT - 1)
                    continue
                full = rounds - 1 if last_phase else rounds
                with se.Fori(0, full) as i:
                    for j in range(4):
                        splits(i, name, j)
                        if tiles == 4 or j % 2:
                            tile_post(name, i, j, j if tiles == 4 else j // 2)
                if last_phase:
                    i = rounds - 1
                    for j in range(4):
                        if j < 3:
                            splits(i, name, j)
                        if tiles == 4 or j % 2:
                            tile_post(name, i, j, j if tiles == 4 else j // 2)
            norm_squares(se, K_FINAL, H_FINAL)
            for g in range(8):
                se.wait_ge(S("row_turned"), g + 1)
                if g >= 2:
                    se.wait_ge(S(f"stored{g % 2}"), 16 * (g // 2))
                A_(row_out[:, g % 2, :], (A, B)[g % 2][:, :]).then_inc(S("row_ready"), 1)

        @block.gpsimd
        def _(gp):
            if "s5in" not in plan:
                return
            gp.dma_start(tcol[:, :], t["constants"][:, C_PAR:C_PAR + 6]).then_inc(S("t_in"), 16)
            gp.dma_start(tw[:, 3, :], t["constants"][:, C_T:C_T + NT]).then_inc(S("tokens_in"), 16)
            gp.wait_ge(S("t_in"), 16)
            gp.wait_ge(S("tokens_in"), 16)
            gp.wait_ge(S("setup_vectors"), 4)
            big = tcol[:, 4:5].to_broadcast([P, NT])
            tokens, rest, whole = tw[:, 3, :], tw[:, 0, :], tw[:, 1, :]

            def turns(ct, r4):
                pi = 4 * ct + r4
                a = r4 % 2
                v = turning[:, a, :]
                at = ds(pi, 1) if not isinstance(ct, int) else slice(pi, pi + 1)
                done = [0]

                def step(ins):
                    ins.then_inc(S("turn_step"), 1)
                    done[0] += 1
                    gp.wait_ge(S("turn_step"), pi * 9 + done[0])

                step(gp.tensor_copy(tq[:, :, :], s5v[:, 1:3, at]))
                if not isinstance(ct, int) or r4 >= 2:
                    gp.wait_ge(S(f"turn_saved{a}"), ct * 32 + 16 * (r4 // 2))
                gp.tensor_tensor(v, tokens, tq[:, 0, :].to_broadcast([P, NT]), ALU.mult)
                step(gp.tensor_tensor(rest, tokens, tq[:, 1, :].to_broadcast([P, NT]), ALU.mult))
                step(gp.tensor_tensor(whole, v, big, ALU.add))
                step(gp.tensor_tensor(whole, whole, big, ALU.subtract))
                step(gp.tensor_tensor(v, v, whole, ALU.subtract))
                step(gp.tensor_tensor(v, v, rest, ALU.add))
                step(gp.tensor_tensor(whole, v, big, ALU.add))
                step(gp.tensor_tensor(whole, whole, big, ALU.subtract))
                step(gp.tensor_tensor(v, v, whole, ALU.subtract))
                dst = turns_dram[ct] if isinstance(ct, int) else turns_dram[ds(ct, 1)][0]
                gp.dma_start(dst[:, r4, :], v).then_inc(S(f"turn_saved{a}"), 16)

            for r4 in range(4):
                turns(0, r4)
            with gp.Fori(1, KT) as ct:
                for r4 in range(4):
                    turns(ct, r4)

            for a in range(2):
                gp.wait_ge(S(f"turn_saved{a}"), 16 * 2 * KT)
            gp.wait_ge(S("h_updated"), 1 + h_done["s5in"])

            def turn_load(ct, hf):
                src = turns_dram[ct] if isinstance(ct, int) else turns_dram[ds(ct, 1)][0]
                gp.dma_start(turn[:, 2 * hf:2 * hf + 2, :], src[:, 2 * hf:2 * hf + 2, :]).then_inc(S(f"turn_in{hf}"), 16)

            for hf in range(2):
                turn_load(0, hf)
            gp.memset(b_blk[:, :, :, :, :].rearrange("p a r g e -> p (a r g e)"), 0.0).then_inc(S("blk_zero"), 1)
            gp.wait_ge(S("blk_zero"), 1)

            def spread(i, j):
                ct = i * 4 + j
                a = j % 2
                gp.wait_ge(S(f"bc_in{a}"), i * 128 + 64 * (j // 2 + 1))
                q4 = ds(i * 16 + 4 * j, 4) if not isinstance(i, int) else slice(16 * i + 4 * j, 16 * i + 4 * j + 4)
                co = [s5v[:, 3 + e, q4].unsqueeze(2).to_broadcast([P, 4, 16]) for e in range(2)]
                for e, (x, y_) in enumerate(((0, 0), (1, 1), (0, 1), (1, 0))):
                    mm = gp.tensor_tensor(b_t[:, e, :].rearrange("p (r e) -> p r e", r=4), b_in[:, a, x, :, :], co[y_], ALU.mult)
                mm.then_inc(S("b_products"), 1)
                gp.wait_ge(S("b_products"), ct + 1)
                gp.wait_ge(S("bc_turned"), 1 + ct)
                for g in range(2):
                    rws = slice(64 * g, 64 * g + 64)
                    bt = lambda e: b_t[rws, e, :].rearrange("p (r e) -> p r e", r=4)
                    gp.tensor_tensor(b_blk[rws, 0, :, g, :], bt(0), bt(1), ALU.subtract)
                    gp.tensor_tensor(b_blk[rws, 1, :, g, :], bt(2), bt(3), ALU.add).then_inc(S("blk_half"), 1)
                    gp.wait_ge(S("blk_half"), ct * 2 + g + 1)
                for e in range(2):
                    mm = gp.tensor_tensor(c_blk[:, e, :, :], c_in[:, a, e, :].unsqueeze(1).to_broadcast([P, 2, 64]),
                                          tcol[:, 2 * e:2 * e + 2].unsqueeze(2).to_broadcast([P, 2, 64]), ALU.mult)
                mm.then_inc(S("spread"), 1)

            def turn_forward(i, j):
                for r4 in range(4):
                    pi = i * 16 + (4 * j + r4)
                    a = r4 % 2
                    gp.wait_ge(S("scanned"), pi + 1)
                    gp.wait_ge(S("y_done"), two_pairs_back(i, j, r4))
                    gp.tensor_tensor(x2[:, a, :, :], st[:, a, :, :], rot[:, a, 2:4, :], ALU.mult).then_inc(S("x2_ready"), 1)
                    if r4 == 2 and ahead(i, j, 2):
                        spread(i, j + 2)
                    if r4 % 2 and ahead(i, j, 1):
                        turn_load(i * 4 + (j + 1), r4 // 2)

            spread(0, 0)
            spread(0, 1)
            s5_rounds(gp, turn_forward)

        @block.vector
        def _(ve):
            for name in ("mid_lo", "o_normed", "x1_ready", "x2_ready", "s5_lo", "gelu_in", "glu_ready", "act_ready", "h_updated", "proj_read", "hidden_lo"):
                ve.sem_inc(S(name), 1)
            link_n = [0]

            def link(ins):
                link_n[0] += 1
                ins.then_inc(S("vector_setup"), 1)
                ve.wait_ge(S("vector_setup"), link_n[0])

            TT, TS, STT = ve.tensor_tensor, ve.tensor_scalar, ve.scalar_tensor_tensor
            ve.wait_ge(S("params_in"), 16 * N_PARAMS)
            ve.tensor_copy(rows[0:64, 4, :].rearrange("p (g q) -> p g q", g=2),
                           ls2[0:64, :].unsqueeze(2).to_broadcast([64, 2, 64])).then_inc(S("steps_ready"), 1)
            for q in range(QUARTERS):
                split_lo(ve, 0, q, 0, 0)
            ve.wait_ge(S("x_squared"), 3)
            link(ve.reciprocal(stat[:, 4:6], stat[:, 2:4]))
            ve.wait_ge(S("x_turned"), 8)
            for b in range(2):
                TS(xn[:, b, :], xn[:, b, :], stat[:, 4 + b:5 + b], None, ALU.mult).then_inc(S("x_scaled"), 1)
            ve.wait_ge(S("ba_hi"), 1)
            TT(mid[:, 2:4, :].rearrange("p a n -> p (a n)"), ba_w[:, :],
               mid[:, 0:2, :].rearrange("p a n -> p (a n)").bitcast(F32), ALU.subtract).then_inc(S("ba_lo"), 1)
            for kt in range(KT):
                ve.wait_ge(S("x_hi"), 2 * (kt // 2) + 2)
                STT(act[:, kt, NT:2 * NT], (C, Dk, E, F)[kt // 2 % 4][:, (kt % 2) * NT:(kt % 2 + 1) * NT],
                    vec[:, V_MIX + kt:V_MIX + kt + 1], act[:, kt, 0:NT].bitcast(F32), ALU.mult,
                    ALU.subtract).then_inc(S("act_ready0"), 1)

            c_ = lambda i: cf[:, i, :]
            s_ = lambda i: s5v[:, i, :]
            ve.wait_ge(S("vectors_ready"), 2)
            TT(c_(4), c_(0), c_(2), ALU.mult).then_inc(S("setup_vectors"), 1)
            link(TT(c_(3), c_(1), c_(2), ALU.mult))
            link(TS(c_(8), c_(3), 1 / TWO_PI_EXACT, MAGIC, ALU.mult, ALU.add))
            link(TS(c_(8), c_(8), MAGIC, None, ALU.subtract))
            link(STT(c_(10), c_(8), -TP1, c_(3), ALU.mult, ALU.add))
            link(STT(c_(10), c_(8), -TP2, c_(10), ALU.mult, ALU.add))
            link(STT(c_(10), c_(8), -TP3, c_(10), ALU.mult, ALU.add))
            TS(c_(10), c_(10), PI_BELOW, -PI_BELOW, ALU.min, ALU.max).then_inc(S("setup_vectors"), 1)
            ve.wait_ge(S("setup_vectors"), 2)
            link(TS(c_(14), c_(10), 1 / TWO_PI_EXACT, 4096.0, ALU.mult, ALU.mult))
            link(TS(c_(14), c_(14), MAGIC, MAGIC, ALU.add, ALU.subtract))
            link(TS(s_(1), c_(14), 1 / 4096.0, None, ALU.mult))
            link(STT(c_(14), s_(1), -TP1, c_(10), ALU.mult, ALU.add))
            link(STT(c_(14), s_(1), -TP2, c_(14), ALU.mult, ALU.add))
            link(STT(c_(14), s_(1), -TP3, c_(14), ALU.mult, ALU.add))
            link(TS(s_(2), c_(14), 1 / TWO_PI_EXACT, None, ALU.mult))
            link(STT(c_(13), c_(10), -1.0, c_(10), ALU.mult, ALU.min))
            TS(c_(13), c_(13), math.pi / 2, None, ALU.add).then_inc(S("setup_vectors"), 1)
            link(TS(c_(6), c_(4), -1.0, 1.0, ALU.max, ALU.min))
            link(TS(c_(6), c_(6), 0.25, None, ALU.mult))
            link(TS(c_(7), c_(6), 1 / 8.0, 1.0, ALU.mult, ALU.add))
            for d in (7, 6, 5, 4, 3, 2):
                link(TT(c_(7), c_(7), c_(6), ALU.mult))
                link(TS(c_(7), c_(7), 1.0 / d, 1.0, ALU.mult, ALU.add))
            link(TT(c_(7), c_(7), c_(6), ALU.mult))
            for _ in range(2):
                link(STT(c_(7), c_(7), 2.0, c_(7), ALU.add, ALU.mult))
            ve.wait_ge(S("setup_functions"), 1)
            link(TS(c_(5), c_(5), 1.0, None, ALU.subtract))
            link(STT(c_(8), c_(4), -1.0, c_(4), ALU.mult, ALU.max))
            link(TS(c_(8), c_(8), 1.0, None, ALU.is_lt))
            link(TT(c_(7), c_(7), c_(5), ALU.subtract))
            link(TT(c_(7), c_(7), c_(8), ALU.mult))
            link(TT(c_(7), c_(7), c_(5), ALU.add))
            link(TS(s_(0), c_(7), 1.0, None, ALU.add))
            ve.wait_ge(S("setup_functions"), 2)
            ve.wait_ge(S("setup_functions"), 3)
            link(TT(c_(12), c_(12), c_(12), ALU.mult))
            link(TT(c_(13), c_(13), c_(7), ALU.mult))
            link(STT(c_(12), c_(12), -2.0, c_(13), ALU.mult, ALU.add))
            link(TT(c_(11), c_(11), s_(0), ALU.mult))
            link(TT(c_(5), c_(0), c_(0), ALU.mult))
            link(TT(c_(6), c_(1), c_(1), ALU.mult))
            link(TT(c_(5), c_(5), c_(6), ALU.add))
            link(ve.reciprocal(c_(5), c_(5)))
            link(TT(c_(6), c_(12), c_(0), ALU.mult))
            link(TT(c_(8), c_(11), c_(1), ALU.mult))
            link(TT(c_(6), c_(6), c_(8), ALU.add))
            link(TT(s_(3), c_(6), c_(5), ALU.mult))
            link(TT(c_(6), c_(11), c_(0), ALU.mult))
            link(TT(c_(8), c_(12), c_(1), ALU.mult))
            link(TT(c_(6), c_(6), c_(8), ALU.subtract))
            TT(s_(4), c_(6), c_(5), ALU.mult).then_inc(S("setup_vectors"), 1)

            gv = lambda i: ga[:, i, :].rearrange("p (b h) -> p b h", b=2)
            ve.wait_ge(S("setup_functions"), 4)
            link(TS(ga[:, 1, :], ga[:, 0, :], 1.0, None, ALU.add))
            link(ve.reciprocal(ga[:, 2, :], ga[:, 1, :]))
            v = A[:, 0:P].rearrange("p (b k h) -> p b k h", b=2, k=2)
            link(TT(gv(3), v[:, :, 1, :], abias[:, 1, :].unsqueeze(1).to_broadcast([P, 2, 32]), ALU.add))
            STT(ga[:, 4, :], ga[:, 3, :], -1.0, ga[:, 3, :], ALU.mult, ALU.max).then_inc(S("setup_vectors"), 1)
            ve.wait_ge(S("setup_functions"), 6)
            TS(ga[:, 5, :], ga[:, 5, :], 1.0, None, ALU.add).then_inc(S("setup_vectors"), 1)
            ve.wait_ge(S("setup_functions"), 7)
            link(STT(ga[:, 7, :], ga[:, 3, :], 0.0, ga[:, 6, :], ALU.max, ALU.add))
            ve.wait_ge(S("setup_functions"), 5)
            STT(gv(8), gv(7), -1.0, abias[:, 2, :].unsqueeze(1).to_broadcast([P, 2, 32]), ALU.mult,
                ALU.mult).then_inc(S("setup_vectors"), 1)
            ve.wait_ge(S("setup_functions"), 8)
            link(ve.tensor_copy(ga[:, 0, :], B[:, 0:64]))
            TT(ga[:, 11, :], B[:, 64:128], ga[:, 0, :], ALU.subtract).then_inc(S("setup_vectors"), 1)
            ve.wait_ge(S("setup_functions"), 8)
            TT(ga[:, 10, :], ga[:, 2, :], ga[:, 9, :], ALU.mult)
            link(TS(ga[:, 4, :], ga[:, 2, :], 0.5, None, ALU.mult))
            ve.wait_ge(S("setup_functions"), 9)
            ve.wait_ge(S("setup_vectors"), 7)
            for b in range(2):
                for col, i in ((H_BETA, 2), (H_GC, 0), (H_BEXP, 10), (H_KD, 11), (H_G, 8), (H_BHALF, 4)):
                    ve.tensor_copy(gt[:, :, col + 2 * b:col + 2 * b + 2],
                                   ga[:, i, 32 * b:32 * b + 32].rearrange("p (i h) -> p i h", h=2))
                for hc in range(2):
                    last = ve.tensor_copy(gt[:, :, H_GLAST + 4 * b + 2 * hc:H_GLAST + 4 * b + 2 * hc + 2],
                                          ga[:, (1, 3)[hc], 32 * b:32 * b + 32].rearrange("p (i h) -> p i h", h=2))
            link(last)
            link(ve.memset(pre[:, :, 0:4], 0.0))
            link(TS(onorm[:, :], onorm[:, :], 0.5 * 128 ** -0.5, None, ALU.mult))
            ve.wait_ge(S("h_saved"), 16)

            def gate(n, par, dst):
                ve.wait_ge(S("tanh_ready"), n + 1)
                STT(dst, tanh[:, par, :], 1.0, dst, ALU.add, ALU.mult).then_inc(S("gated"), 1)

            def front(hd, j):
                n, fi = 6 * hd + j, 4 * hd + j
                sum_halves(ve, n, j % 2, pre[:, j, 3:NT + 3])
                tile = (hd, hd + 16, 2 * hd + 32, 2 * hd + 33)[j]
                at = ds(tile, 1) if not isinstance(tile, int) else slice(tile, tile + 1)
                ve.tensor_copy(conv_f[:, j, :].unsqueeze(2), conv_w[:, :, at]).then_inc(S("taps_ready"), 1)
                ve.wait_ge(S("acc_freed"), n + 1)
                ve.wait_ge(S("taps_ready"), fi + 1)
                TS(y[:, j, :], pre[:, j, 0:NT], conv_f[:, j, 0:1], None, ALU.mult).then_inc(S("tap_added"), 1)
                for k in range(1, 4):
                    ve.wait_ge(S("tap_added"), 3 * fi + k)
                    ins = STT(y[:, j, :], pre[:, j, k:k + NT], conv_f[:, j, k:k + 1], y[:, j, :], ALU.mult, ALU.add)
                    ins.then_inc(S("tap_added" if k < 3 else "conv_done"), 1)
                gate(n, j % 2, y[:, j, :])

            def front_z(r, j):
                n = 6 * r + 4 + j
                sum_halves(ve, n, j, z[:, j, :])
                gate(n, j, z[:, j, :])

            for n in range(4):
                for q in range(QUARTERS):
                    split_lo(ve, n + 1, q, (n + 1) % 3, (n + 1) % 2)
                if n < 3:
                    front(0, n)

            def scalars(r):
                at = ds(r, 1) if not isinstance(r, int) else slice(r, r + 1)
                ve.tensor_copy(hs[:, :].unsqueeze(1), gt[:, at, :]).then_inc(S("hs_ready"), 1)

            def unit_qk(r):
                ve.wait_ge(S("qk_inverse"), r + 1)
                ve.wait_ge(S("gated"), 6 * r + 2)
                STT(qkn[:, :, :].rearrange("p m q -> p (m q)"), y[:, 0:2, :].rearrange("p a n -> p (a n)"), 0.5,
                    rn[:, :, :].rearrange("p m q -> p (m q)"), ALU.mult, ALU.mult).then_inc(S("qkn_ready"), 1)

            def core(r, s):
                w = lambda name, k=1, o=1: ve.wait_ge(S(name), k * r + o)
                fl = lambda a: a[:, :, :].rearrange("p m q -> p (m q)")
                hcol = lambda c: hs[:, c:c + 1]
                bh = lambda a: a[:, :, :].rearrange("p (b h) q -> p b h q", b=2)
                if s == 0:
                    w("mid_lo")
                    w("gcrow")
                    w("erow_ready")
                    w("hs_ready")
                    for m in range(4):
                        last = TS(D1[:, m, :], C[:, m * P:(m + 1) * P], hcol(H_GC + m), 0.0, ALU.subtract, ALU.max)
                    last.then_inc(S("d1_ready"), 1)
                    for m in range(4):
                        last = TS(qkT[:, m, :], C[:, m * P:(m + 1) * P], hcol(H_GC + m), 0.0, ALU.subtract, ALU.min)
                    last.then_inc(S("d2_ready"), 1)
                elif s == 2:
                    w("attn_done")
                    w("D1_ready")
                    for m in range(4):
                        b = m // 2
                        last = STT(Mp[:, m, :], B[:, b * NT + P:b * NT + 2 * P], hcol(H_BETA + m), D1[:, m, :],
                                   ALU.mult, ALU.mult)
                    last.then_inc(S("M_ready"), 1)
                    w("M_ready")
                    mk = lambda k: masks[:, k, :].unsqueeze(1).to_broadcast([P, 4, P])
                    TT(Pm[:, :, :], Mp[:, :, :], mk(2), ALU.mult).then_inc(S("P_ready"), 1)
                    TT(L1[:, :, :], Mp[:, :, :], mk(3), ALU.mult)
                    TT(L2[:, :, :], Mp[:, :, :], mk(4), ALU.mult).then_inc(S("L_ready"), 1)
                elif s == 3:
                    w("PT_ready")
                    TT(RT[:, :, :], PT[:, :, :],
                       ident.unsqueeze(1).to_broadcast([P, 4, P]), ALU.add).then_inc(S("RT_ready"), 1)
                    w("D2_ready")
                    qk = B[:, :].rearrange("p (b a q) -> p b a q", b=2, a=2)[:, :, 0:1, :].to_broadcast([P, 2, 2, P])
                    TT(bh(qkT), bh(qkT), qk, ALU.mult).then_inc(S("qk_decay"), 1)
                    w("qk_decay")
                    TT(qkT[:, :, :], qkT[:, :, :], U.unsqueeze(1).to_broadcast([P, 4, P]), ALU.mult).then_inc(S("qkT_ready"), 1)
                    w("erow_ready")
                    w("qkn_ready")
                    qn = qkn[:, 0:2, :].unsqueeze(2).to_broadcast([P, 2, 2, P])
                    TT(bh(qeT), qn, bh(erow), ALU.mult).then_inc(S("qeT_ready"), 1)
                elif s == 4:
                    w("P2T_done")
                    w("qeT_ready")
                    ve.tensor_copy(fl(P2T), F[:, :]).then_inc(S("P2T_ready"), 1)
                elif s in (5, 6, 7):
                    i = s - 4
                    w("R_done", 5, i)
                    w("RT_ready", 6, i)
                    TT(fl(RT), A[:, :], fl(RT), ALU.add).then_inc(S("RT_ready"), 1)
                    if s == 5:
                        w("P4T_done")
                        ve.tensor_copy(fl(P4T), F[:, :]).then_inc(S("P4T_ready"), 1)
                elif s in (10, 12):
                    i = 4 if s == 10 else 5
                    w("R_done", 5, i)
                    w("RT_ready", 6, i)
                    TT(fl(RT), fl(RT), C[:, :], ALU.subtract).then_inc(S("RT_ready"), 1)
                elif s == 13:
                    w("U_done")
                    ve.tensor_copy(fl(VN), A[:, :]).then_inc(S("VN_ready"), 1)
                elif s == 14:
                    ve.wait_ge(S("kv_done"), 3 * r + 1)
                    ve.tensor_copy(fl(state), C[:, 0:2 * P]).then_inc(S("state_ready"), 1)
                elif s in (15, 17, 19):
                    c = (s - 13) // 2
                    b, lo = c // 2, 64 * (c % 2)
                    ve.wait_ge(S("ws_done"), 3 * r + c)
                    w("VN_ready")
                    dst = VN[lo:lo + 64, 2 * b:2 * b + 2, :].rearrange("p m q -> p (m q)")
                    TT(dst, dst, A[lo:lo + 64, 0:2 * P], ALU.add).then_inc(S("vn_ready"), 1)
                elif s in (16, 18):
                    c = (s - 14) // 2
                    ve.wait_ge(S("kv_done"), 3 * r + c + 1)
                    ve.wait_ge(S("state_ready"), 3 * r + c)
                    for hd in range(2):
                        last = STT(state[:, hd, :], state[:, hd, :], hcol(H_GLAST + 2 * c + hd), C[:, hd * P:(hd + 1) * P],
                                   ALU.mult, ALU.add)
                    last.then_inc(S("state_ready"), 1)
                elif s == 22:
                    w("o_inverse")
                    TT(fl(oy), B[:, :], fl(orn), ALU.mult).then_inc(S("o_normed"), 1)
                    w("o_normed", 1, 2)
                    ve.wait_ge(S("gated"), 6 * r + 6)
                    STT(fl(oy), fl(oy), onorm[:, 0:1], z[:, :, :].rearrange("p a n -> p (a n)"), ALU.mult,
                        ALU.mult).then_inc(S("oy_ready"), 1)
                    w("oy_ready")
                    w("mid_hi")
                    at = ds(2 * r, 2) if not isinstance(r, int) else slice(2 * r, 2 * r + 2)
                    TT(mid[:, at, NT:2 * NT], oy[:, :, :].rearrange("p (a m) q -> p a (m q)", a=2),
                       mid[:, at, 0:NT].bitcast(F32), ALU.subtract).then_inc(S("mid_lo"), 1)

            def head(r, last):
                for s in range(24):
                    if s < 8 or not last:
                        m = 5 + s // 4
                        split_lo(ve, 6 * r + m, s % 4, 0 if last and m == 6 else m % 3, m % 2)
                    if s == 20 and not last:
                        unit_qk(r + 1)
                    if s in (4, 8):
                        front_z(r, s // 4 - 1)
                    if s in (12, 16, 20) and not last:
                        front(r + 1, s // 4 - 3)
                    core(r, s)
                    if s == 0:
                        front(r, 3)
                    if s == 19 and not last:
                        ve.wait_ge(S("state_ready"), 3 * r + 3)
                        scalars(r + 1)

            scalars(0)
            unit_qk(0)
            with ve.Fori(0, KH - 1) as r:
                head(r, False)
            head(KH - 1, True)

            def tile_post(name, i, j, tj):
                n0, t0, rounds, chunks, tiles = plan[name]
                tau = i * tiles + (t0 + tj)
                a = tj % 2
                if name[:2] == "up":
                    tile = 32 * (2 * int(name[2]) + int(name[3])) + j + 1
                    sum_halves(ve, tau, a, summed[:, a, :])
                    ve.wait_ge(S("acc_freed"), tau + 1)
                    ve.wait_ge(S("hidden_lo"), i * 4 + max(tile - 1, 1))
                    STT(normed[:, a, :], summed[:, a, :], 0.0, summed[:, a, :], ALU.max, ALU.mult).then_inc(S("hidden"), 1)
                    ve.wait_ge(S("hidden_hi"), i * 4 + tile)
                    TT(mid[:, ds(i * 4 + j, 1), NT:2 * NT], normed[:, a, :],
                       mid[:, ds(i * 4 + j, 1), 0:NT].bitcast(F32), ALU.subtract).then_inc(S("hidden_lo"), 1)
                elif name[:3] == "ple":
                    sum_halves(ve, tau, a, summed[:, a, :])
                    ct = i * 4 + (16 * int(name[3]) + j)
                    ve.wait_ge(S("projected"), ct + 1)
                    ve.wait_ge(S("h_updated"), 1 + i * 4 + (h_done[name] + j))
                    ve.wait_ge(S("gate_tanh"), ct + 1)
                    STT(normed[:, a, :], tanh[:, a, :], 1.0, (C, Dk)[a][:, 0:NT], ALU.add, ALU.mult).then_inc(S("proj_read"), 1)
                    ve.wait_ge(S("proj_read"), 1 + ct + 1)
                    hv = h[:, ds(i * 4 + j, 1), :]
                    STT(hv, normed[:, a, :], 0.5, hv, ALU.mult, ALU.add).then_inc(S("h_updated"), 1)
                elif name == "s5out":
                    if not a:
                        ve.wait_ge(S("glu_ready"), 1 + i * 2 + j // 2)
                    sum_halves(ve, tau, a, summed[:, a, :])
                    if a:
                        pair = i * 2 + j // 2
                        ve.wait_ge(S("glu_tanh"), pair + 1)
                        ve.wait_ge(S("h_updated"), 1 + i * 2 + (h_done[name] + j // 2))
                        STT(normed[:, 0, :], tanh[:, 1, :], 1.0, summed[:, 0, :], ALU.add, ALU.mult).then_inc(S("glu_ready"), 1)
                        ve.wait_ge(S("glu_ready"), 1 + pair + 1)
                        hv = h[:, ds(i * 2 + j // 2, 1), :]
                        STT(hv, normed[:, 0, :], 0.5, hv, ALU.mult, ALU.add).then_inc(S("h_updated"), 1)
                else:
                    ve.wait_ge(S("h_updated"), 1 + i * 2 + (h_done[name] + tj))
                    sum_halves(ve, tau, a, summed[:, a, :])
                    ve.wait_ge(S("acc_freed"), tau + 1)
                    hv = h[:, ds(i * 2 + tj, 1), :]
                    TT(hv, hv, summed[:, a, :], ALU.add).then_inc(S("h_updated"), 1)

            one = lambda x: ds(x, 1) if not isinstance(x, int) else slice(x, x + 1)

            def turn_forward(pi, r4, before):
                ve.wait_ge(S("scanned"), pi + 1)
                ve.wait_ge(S("x1_used"), before)
                TT(x1[:, r4 % 2, :, :], st[:, r4 % 2, :, :], rot[:, r4 % 2, 0:1, :].to_broadcast([P, 2, NT]),
                   ALU.mult).then_inc(S("x1_ready"), 1)

            def gelu(step, ct, par):
                if step == 0:
                    ve.wait_ge(S("y_done"), ct * 4 + 5)
                    ve.wait_ge(S("s5_lo"), ct + 1)
                    STT(gl[:, 0, :], u[:, par, :], vec[:, one(ct + V_D)], A[:, 0:NT], ALU.mult,
                        ALU.add).then_inc(S("gelu_in"), 1)
                elif step == 1:
                    ve.wait_ge(S("gelu_sq"), ct + 1)
                    TS(gl[:, 1, :], gl[:, 1, :], 0.044715, 1.0, ALU.mult, ALU.add).then_inc(S("gelu_poly"), 1)
                elif step == 2:
                    ve.wait_ge(S("gelu_poly"), ct + 1)
                    TT(gl[:, 1, :], gl[:, 1, :], gl[:, 0, :], ALU.mult).then_inc(S("gelu_arg"), 1)
                elif step == 3:
                    ve.wait_ge(S("gelu_tanh"), ct + 1)
                    STT(gl[:, 0, :], gl[:, 1, :], 1.0, gl[:, 0, :], ALU.add, ALU.mult).then_inc(S("gelu_ready"), 1)
                else:
                    ve.wait_ge(S("s5_hi"), ct + 1)
                    STT(mid[:, one(ct), NT:2 * NT], gl[:, 0:1, :], 0.5, mid[:, one(ct), 0:NT].bitcast(F32), ALU.mult,
                        ALU.subtract).then_inc(S("s5_lo"), 1)

            def s5_tile(i, j):
                n0, t0 = plan["s5in"][0:2]
                ct = i * 4 + j
                for r4 in range(4):
                    pi = i * 16 + (4 * j + r4)
                    X = (C, Dk, E, F)[r4][:, :].rearrange("p (a n) -> p a n", a=2)
                    a = r4 % 2
                    before = two_pairs_back(i, j, r4)
                    ve.wait_ge(S("rot_ready"), pi + 2)
                    ve.wait_ge(S("bu_done"), pi + 1)
                    ve.wait_ge(S("x1_ready"), before)
                    ve.wait_ge(S("x2_ready"), before)
                    TT(st[:, a, :, :], X, rot[:, a, 0:1, :].to_broadcast([P, 2, NT]), ALU.mult)
                    TT(rb[:, :, :], X, rot[:, a, 1:3, :], ALU.mult).then_inc(S("bu_products"), 1)
                    if ahead(i, j, 2):
                        split_lo(ve, ct + (n0 + 3), r4, (j + 3) % 4, (j + 1) % 2)
                    ve.wait_ge(S("bu_products"), pi + 1)
                    TT(st[:, a, 0, :], st[:, a, 0, :], rb[:, 1, :], ALU.add)
                    TT(st[:, a, 1, :], st[:, a, 1, :], rb[:, 0, :], ALU.add).then_inc(S("bu_turned"), 1)
                    if r4 or ahead(i, j, -1):
                        turn_forward(pi - 1, (r4 + 3) % 4, two_pairs_back(i, j, r4 - 1))
                    if r4 == 0 and ahead(i, j, -2):
                        gelu(4, ct - 2, None)
                    if r4 == 1:
                        if ahead(i, j, -1):
                            gelu(0, ct - 1, (j + 1) % 2)
                        if ahead(i, j, 1):
                            ve.wait_ge(S("gelu_in"), ct + 1)
                            sum_halves(ve, ct + (t0 + 1), (j + 1) % 2, u[:, (j + 1) % 2, :])
                    if r4 >= 2 and ahead(i, j, -1):
                        gelu(2 * r4 - 3, ct - 1, None)
                    ve.wait_ge(S("bu_turned"), pi + 1)
                    decay = s5v[:, 0, one(pi)].to_broadcast([P, NT])
                    for e in range(2):
                        last = ve.tensor_tensor_scan(st[:, a, e, :], decay, st[:, a, e, :], 0.0, ALU.mult, ALU.add)
                    last.then_inc(S("scanned"), 1)
                    if r4 == 2 and ahead(i, j, -1):
                        gelu(2, ct - 1, None)

            def splits(i, name, j):
                n0 = plan[name][0]
                for q in range(QUARTERS):
                    split_lo(ve, i * 4 + (n0 + j + 1), q, (j + 1) % 4, (j + 1) % 2)

            for name, (n0, t0, rounds, chunks, tiles) in plan.items():
                last_phase = name == list(plan)[-1]
                if name == "gout":
                    ve.wait_ge(S("h_loaded"), 16)
                elif h_done[name]:
                    ve.wait_ge(S("h_updated"), 1 + h_done[name])
                if name in norm_of:
                    norm_apply_vector(ve, norm_of[name], gain_of[name])
                if name == "s5in":
                    for c in (1, 2):
                        for q in range(QUARTERS):
                            split_lo(ve, n0 + c, q, c, c % 2)
                        if c == 1:
                            sum_halves(ve, t0, 0, u[:, 0, :])
                    s5_rounds(ve, s5_tile)
                    turn_forward(4 * KT - 1, 3, 4 * KT - 1)
                    gelu(4, KT - 2, None)
                    for step in range(5):
                        gelu(step, KT - 1, 1)
                    continue
                with ve.Fori(0, rounds - 1 if last_phase else rounds) as i:
                    for j in range(4):
                        splits(i, name, j)
                        if tiles == 4 or j % 2:
                            tile_post(name, i, j, j if tiles == 4 else j // 2)
                if last_phase:
                    for j in range(4):
                        if j < 3:
                            splits(rounds - 1, name, j)
                        if tiles == 4 or j % 2:
                            tile_post(name, rounds - 1, j, j if tiles == 4 else j // 2)
            ve.wait_ge(S("h_updated"), 1 + H_FINAL)
            ve.wait_ge(S("rms_ready"), K_FINAL + 1)
            for kt in range(KT):
                STT(h[:, kt, :], h[:, kt, :], vec[:, V_FIN + kt:V_FIN + kt + 1], rms[:, :], ALU.mult,
                    ALU.mult).then_inc(S("final_ready"), 1)


_INS = ["x", "p", "norm_mix", "norm_mlp", "norm_ple", "norm_final", "gdn_w_in", "gdn_conv_w", "gdn_a_log",
        "gdn_dt_bias", "gdn_o_norm", "gdn_w_out", "s5_w_in", "s5_lam_re", "s5_lam_im", "s5_log_step", "s5_b_re",
        "s5_b_im", "s5_c_re", "s5_c_im", "s5_d", "s5_w_out", "mlp_w_up", "mlp_w_down", "ple_w_proj", "ple_w_gate"]


def _constants():
    import numpy as np
    i = np.arange(P)
    row, col = i[:, None], i[None, :]
    same = row // 64 == col // 64
    below = row > col
    s32, s16 = row // 32 == col // 32, row // 16 == col // 16
    parts = [row == col, np.ones((P, P)), (row <= col) & same, same, -1.0 * (below & s16), below & s32 & ~s16,
             below & same & ~s32, np.broadcast_to(row < 64, (P, P)), np.broadcast_to(row >= 64, (P, P)),
             np.broadcast_to(np.arange(NT), (P, NT))]
    odd = (row // 16) % 2
    parts += [1 - odd, odd, odd - 1, -odd, np.full((P, 1), MAGIC), np.full((P, 1), math.pi / 2), np.full((P, 1), EPS)]
    return np.ascontiguousarray(np.concatenate([np.asarray(a, np.float32) for a in parts], axis=1))


def kernel(**inputs):
    import numpy as _np
    import concourse.bacc as _bacc
    from concourse import mybir as _mybir
    from concourse.bass_utils import run_bass_kernel_spmd as _run

    nc = _bacc.Bacc("TRN2", target_bir_lowering=False, num_devices=1)
    arrays, tensors = {}, {}
    for name in _INS + ["constants"]:
        a = _constants() if name == "constants" else _np.ascontiguousarray(inputs[name])
        arrays[f"in_{name}_dram"] = a
        tensors[name] = nc.dram_tensor(f"in_{name}_dram", a.shape, _mybir.dt.from_np(a.dtype), kind="ExternalInput").ap()
    out = nc.dram_tensor("out_0_dram", (1, NT, D), _mybir.dt.float32, kind="ExternalOutput").ap()
    trunk(nc, tensors, out)
    r = _run(nc, [arrays], core_ids=[0])
    return r.results[0]["out_0_dram"]
```
